# Optimizing a Trainium2 kernel written in Bass

```python
import jax, jax.numpy as jnp
from jax import lax
import numpy as np

D_MODEL = 2048
BATCH = 1
SEQ = 256
DEPTH = 2

HEAD_DIM = 128
D_ATT = D_MODEL // 2
N_HEADS_ATT = D_ATT // HEAD_DIM
Q_BLOCK = 128
D_SC = D_MODEL // 4
N_GROUPS_SC = 4
SC_WIDTH = 3
D_CF = D_MODEL // 4
N_GROUPS_CF = 4
CF_WIDTH = 31
N_BRANCH = 3
D_FF = 4 * D_MODEL
N_IN = 3 * D_ATT + 3 * D_SC + 2 * D_CF + N_BRANCH * D_MODEL
RMS_EPS = 1e-6
LN_EPS = 1e-5

kernel_name = 'gated_parallel_hybrid_sb_conv_block'

def rms_norm(x, g):
    xf = x.astype(jnp.float32)
    y = xf * lax.rsqrt(jnp.mean(jnp.square(xf), axis=-1, keepdims=True) + RMS_EPS)
    return (y * g.astype(jnp.float32)).astype(x.dtype)

def layer_norm(x, g, b):
    xf = x.astype(jnp.float32)
    mu = jnp.mean(xf, axis=-1, keepdims=True)
    var = jnp.mean(jnp.square(xf - mu), axis=-1, keepdims=True)
    y = (xf - mu) * lax.rsqrt(var + LN_EPS)
    return (y * g.astype(jnp.float32) + b.astype(jnp.float32)).astype(x.dtype)

def causal_dwconv(u, w):
    K, C = w.shape
    return lax.conv_general_dilated(
        u, w[:, None, :].astype(u.dtype), window_strides=(1,), padding=[(K - 1, 0)],
        dimension_numbers=('NWC', 'WIO', 'NWC'), feature_group_count=C)

def stick_breaking_attention(q, k, v):
    S = q.shape[1]
    scale = HEAD_DIM ** -0.5
    outs = []
    for blk in range(S // Q_BLOCK):
        q0 = blk * Q_BLOCK
        kend = q0 + Q_BLOCK
        qb = q[:, q0:kend]
        kb = k[:, :kend]
        vb = v[:, :kend]
        z = jnp.einsum('bthd,bshd->bhts', qb, kb).astype(jnp.float32) * scale
        t_idx = q0 + jnp.arange(Q_BLOCK)[:, None]
        s_idx = jnp.arange(kend)[None, :]
        mask = s_idx < t_idx
        log_fail = jnp.where(mask, jax.nn.log_sigmoid(-z), 0.0)
        suffix = lax.cumsum(log_fail, axis=3, reverse=True) - log_fail
        log_a = jax.nn.log_sigmoid(z) + suffix
        a = jnp.where(mask, jnp.exp(log_a), 0.0)
        outs.append(jnp.einsum('bhts,bshd->bthd', a.astype(v.dtype), vb))
    return jnp.concatenate(outs, axis=1)

def setup_inputs(seed: int = 0) -> dict:
    key = jax.random.key(seed)
    ks = jax.random.split(key, 20)
    f32 = jnp.float32

    def nrm(k, shape, fan_in):
        return jax.random.normal(k, shape, f32) * (fan_in ** -0.5)

    def gain(k, shape):
        return jnp.ones(shape, f32) + 0.02 * jax.random.normal(k, shape, f32)

    return {
        'x': jax.random.normal(ks[0], (BATCH, SEQ, D_MODEL), f32),
        'ln_mix_pre': gain(ks[1], (DEPTH, D_MODEL)),
        'ln_mix_post': gain(ks[2], (DEPTH, D_MODEL)),
        'ln_mlp_pre': gain(ks[3], (DEPTH, D_MODEL)),
        'ln_mlp_post': gain(ks[4], (DEPTH, D_MODEL)),
        'w_in': nrm(ks[5], (DEPTH, D_MODEL, N_IN), D_MODEL),
        'conv_a_w': nrm(ks[6], (DEPTH, SC_WIDTH, D_SC), SC_WIDTH),
        'proj_a': nrm(ks[7], (DEPTH, D_SC, D_MODEL), D_SC),
        'proj_b': nrm(ks[8], (DEPTH, D_ATT, D_MODEL), D_ATT),
        'conv_c_w': nrm(ks[9], (DEPTH, CF_WIDTH, D_CF), CF_WIDTH),
        'conv_c_b': 0.02 * jax.random.normal(ks[10], (DEPTH, D_CF), f32),
        'norm_c_g': gain(ks[11], (DEPTH, D_CF)),
        'norm_c_b': 0.02 * jax.random.normal(ks[12], (DEPTH, D_CF), f32),
        'proj_c': nrm(ks[13], (DEPTH, D_CF, D_MODEL), D_CF),
        'w_o': nrm(ks[14], (DEPTH, D_MODEL, D_MODEL), D_MODEL),
        'w_up': nrm(ks[15], (DEPTH, D_MODEL, D_FF), D_MODEL),
        'w_down': nrm(ks[16], (DEPTH, D_FF, D_MODEL), D_FF),
    }

def reference(x, ln_mix_pre, ln_mix_post, ln_mlp_pre, ln_mlp_post, w_in, conv_a_w, proj_a,
              proj_b, conv_c_w, conv_c_b, norm_c_g, norm_c_b, proj_c, w_o, w_up, w_down):
    Bsz, S, _ = x.shape
    sizes = [D_ATT, D_ATT, D_ATT, D_SC, D_SC, D_SC, 2 * D_CF, N_BRANCH * D_MODEL]
    splits = [int(c) for c in np.cumsum(sizes)[:-1]]
    for l in range(DEPTH):
        h = rms_norm(x, ln_mix_pre[l])
        proj = h @ w_in[l]
        q, k, v, sc_b, sc_c, sc_u, cf_in, gate_logits = jnp.split(proj, splits, axis=-1)
        ya = (sc_b * causal_dwconv(sc_c * sc_u, conv_a_w[l])) @ proj_a[l]
        q = q.reshape(Bsz, S, N_HEADS_ATT, HEAD_DIM)
        k = k.reshape(Bsz, S, N_HEADS_ATT, HEAD_DIM)
        v = v.reshape(Bsz, S, N_HEADS_ATT, HEAD_DIM)
        yb = stick_breaking_attention(q, k, v).reshape(Bsz, S, D_ATT) @ proj_b[l]
        cf_a, cf_g = jnp.split(cf_in, 2, axis=-1)
        u = cf_a * jax.nn.sigmoid(cf_g)
        u = causal_dwconv(u, conv_c_w[l]) + conv_c_b[l]
        u = jax.nn.silu(layer_norm(u, norm_c_g[l], norm_c_b[l]))
        yc = u @ proj_c[l]
        g_a, g_b, g_c = jnp.split(jax.nn.sigmoid(gate_logits), N_BRANCH, axis=-1)
        mixed = (g_a * ya + g_b * yb + g_c * yc) @ w_o[l]
        x = x + rms_norm(mixed, ln_mix_post[l])
        h = rms_norm(x, ln_mlp_pre[l])
        f = jnp.square(jax.nn.relu(h @ w_up[l])) @ w_down[l]
        x = x + rms_norm(f, ln_mlp_post[l])
    return x


_drawn_inputs = setup_inputs


def setup_inputs(seed=0):
    import zlib

    import numpy as np

    out = dict(_drawn_inputs(seed))
    spreads = {}
    factors = {'ln_mix_post': 2.741,
     'ln_mlp_pre': 3.016,
     'ln_mlp_post': 9.884,
     'norm_c_g': 5.07,
     'norm_c_b': 5.972}
    for name, (base, spread) in spreads.items():
        noise = np.random.default_rng([zlib.crc32(name.encode()), seed]).standard_normal(out[name].shape)
        drawn = base * np.exp(spread * noise) if base else spread * noise
        out[name] = __import__('jax').numpy.asarray(drawn.astype(out[name].dtype))
    for name, factor in factors.items():
        out[name] = (out[name] * factor).astype(out[name].dtype)
    return out
```

```python
from contextlib import ExitStack

import numpy as np

import concourse.bass as bass
import concourse.mybir as mybir

F32 = mybir.dt.float32
F32R = mybir.dt.float32r
ALU = mybir.AluOpType
ACT = mybir.ActivationFunctionType

P = 128
T = 256
D = 2048
DEPTH = 2
HEADS, HD = 8, 128
D_ATT, D_SC, D_CF, D_FF = D // 2, D // 4, D // 4, 4 * D
TAPS_A, TAPS_C = 3, 31
RMS_EPS, LN_EPS = 1e-6, 1e-5
SCALE = HD ** -0.5
NT = D // P
GT = 4
NG = NT // GT
GW = GT * T
KK = 4
CW = KK * GT * P
PAIRS = HEADS // 2
ZW = T + P
BIG = 3e38

G_MIX_PRE, G_MIX_POST, G_MLP_PRE, G_MLP_POST = 0, NT, 2 * NT, 3 * NT
W_A = 4 * NT
W_C = W_A + GT * TAPS_A
B_C = W_C + GT * TAPS_C
G_LN = B_C + GT
B_LN = G_LN + GT
NPAR = B_LN + GT

C_RMS, C_LN, C_NU, C_NO, C_MASK, C_BOUND = 0, P, 2 * P, 3 * P, 4 * P, 5 * P
NCONST = 5 * P + ZW

R_HEAD = 11
R_MIX = 4 * NG
R_OUT = NG
R_MLP = 2 * NG * NG
ROUNDS = R_HEAD + R_MIX + R_OUT + R_MLP
CHUNKS = 4 * ROUNDS
USES = (32, 31)
TAP_PLAN = {1: (0, 0, 3), 2: (2, 2, 2), 3: (2, 2, 2), 4: (2, 2, 2), 5: (2, 2, 2), 6: (2, 2, 0)}


def build(nc, w_stream, x_in, params_in, consts_in, y_out):
    ctx = ExitStack()
    with ctx:
        def sem(name):
            return ctx.enter_context(nc.semaphore(name))

        KB = 1024
        slab = ctx.enter_context(nc.sbuf_tensor("slab", [P, 206 * KB // 4], F32))
        base = nc.lookup_mloc(slab).addr
        taken = [0]

        def region(size):
            at = taken[0]
            taken[0] += size
            assert taken[0] <= 206 * KB
            return at

        def at(name, shape, dt, offset):
            return nc.alloc_sbuf_tensor_at(name, shape, dt, offset=base + offset)

        raw = at("raw", [P, 4, CW], F32, region(32 * KB))
        w_hi = at("w_hi", [P, 2, CW], F32R, region(16 * KB))
        w_lo = at("w_lo", [P, 2, CW], F32R, region(16 * KB))
        x = at("x_res", [P, NT, T], F32, region(16 * KB))
        h_hi = at("h_hi", [P, NT, T], F32R, region(16 * KB))
        h_lo = at("h_lo", [P, NT, T], F32R, region(16 * KB))

        m = region(32 * KB)
        mid_hi = at("mid_hi", [P, NT, T], F32R, m)
        mid_lo = at("mid_lo", [P, NT, T], F32R, m + 16 * KB)
        q = at("q", [P, HEADS, T], F32, m)
        k = at("k", [P, HEADS, T], F32, m + 8 * KB)
        v = at("v", [P, 2, D_ATT], F32, m + 16 * KB)
        att = at("att", [P, 2, ZW], F32, m + 24 * KB)
        soft = at("soft", [P, 2, ZW], F32, m + 27 * KB)

        r = region(32 * KB)
        ya_hi = at("ya_hi", [P, GT, T], F32R, r)
        ya_lo = at("ya_lo", [P, GT, T], F32R, r + 4 * KB)
        yc_hi = at("yc_hi", [P, GT, T], F32R, r + 8 * KB)
        yc_lo = at("yc_lo", [P, GT, T], F32R, r + 12 * KB)
        yb_hi = at("yb_hi", [P, HEADS, T], F32R, r + 16 * KB)
        yb_lo = at("yb_lo", [P, HEADS, T], F32R, r + 24 * KB)
        y = at("y_sub", [P, NT, T], F32, r)
        factor = at("factor", [P, GW], F32, r)
        ln_work = at("ln_work", [P, GW], F32, r + 4 * KB)

        g = region(20 * KB)
        slot = at("slot", [P, 5, GW], F32, g)
        PAD_C, PAD_A = TAPS_C - 1, TAPS_A - 1
        glu_pad = at("glu_pad", [P, GT, PAD_C + T], F32, g)
        conv_c = at("conv_c", [P, GT, T], F32, g + 4608)
        cu_pad = at("cu_pad", [P, GT, PAD_A + T], F32, g + 8704)
        conv_a = at("conv_a", [P, GT, T], F32, g + 12864)

        var = at("var", [P, T], F32, region(KB))
        rstd = at("rstd", [P, T], F32, region(KB))
        newton = at("newton", [P, T], F32, region(KB))
        consts = at("consts", [P, NCONST], F32, region(4 * NCONST))
        par_all = at("par_all", [P, DEPTH * NPAR], F32, region(4 * DEPTH * NPAR))
        par = at("par", [P, NPAR], F32, region(4 * NPAR))

        ps = ctx.enter_context(nc.psum_tensor("ps", [P, 8, 512], F32))

        def buf(b):
            return ps[:, 2 * b:2 * b + 2, :].rearrange("p b c -> p (b c)")

        scores = ps[:, 4:6, 0:ZW]
        att_out = ps[:, 6, :]
        stat = ps[:, 7, 0:T]

        def tiles(ap):
            return ap.rearrange("p (i t) -> p i t", t=T)

        def over_tiles(ap):
            return ap.unsqueeze(1).to_broadcast([P, GT, T])

        raw_landed = [sem(f"raw_landed{c}") for c in range(4)]
        x_landed = sem("x_landed")
        small_landed = sem("small_landed")
        hi_ready = sem("hi_ready")
        lo_ready = sem("lo_ready")
        chunk_used = sem("chunk_used")
        buf_free = [sem("buf0_free"), sem("buf1_free")]
        par_ready = sem("par_ready")
        squares_ready = sem("squares_ready")
        sum_ready = sem("sum_ready")
        stat_full = sem("stat_full")
        var_ready = sem("var_ready")
        rstd_guess = sem("rstd_guess")
        h_float = sem("h_float")
        h_hi_ready = sem("h_hi_ready")
        h_ready = sem("h_ready")
        x_ready = sem("x_ready")
        gate_sig = sem("gate_sig")
        qkv_ready = sem("qkv_ready")
        conv_c_ready = sem("conv_c_ready")
        mean_full = sem("mean_full")
        centred = sem("centred")
        ln_squared = sem("ln_squared")
        ln_ready = sem("ln_ready")
        ln_sig = sem("ln_sig")
        silu_ready = sem("silu_ready")
        yc_hi_ready = sem("yc_hi_ready")
        yc_ready = sem("yc_ready")
        sc_c_ready = sem("sc_c_ready")
        ya_float = sem("ya_float")
        ya_hi_ready = sem("ya_hi_ready")
        ya_ready = sem("ya_ready")
        scores_full = sem("scores_full")
        softplus_log = sem("softplus_log")
        softplus_ready = sem("softplus_ready")
        log_a_full = sem("log_a_full")
        log_a_ready = sem("log_a_ready")
        att_ready = sem("att_ready")
        out_full = sem("out_full")
        yb_hi_ready = sem("yb_hi_ready")
        yb_ready = sem("yb_ready")
        gate_ready = sem("gate_ready")
        gates_free = sem("gates_free")
        mixed_float = sem("mixed_float")
        mixed_hi_ready = sem("mixed_hi_ready")
        mixed_ready = sem("mixed_ready")
        y_added = sem("y_added")
        relu_free = sem("relu_free")
        f_hi_ready = sem("f_hi_ready")
        f_ready = sem("f_ready")
        stored = sem("stored")

        block = ctx.enter_context(nc.Block())

        @block.sync
        def _(sp):
            for n in range(NG):
                sp.dma_start(x[:, n * GT:(n + 1) * GT, :], x_in[:, n * GT:(n + 1) * GT, :]).then_inc(x_landed, 16)
            for c in range(4):
                sp.dma_start(raw[:, c, :], w_stream[c]).then_inc(raw_landed[c], 16)
            with sp.Fori(1, DEPTH * ROUNDS) as rnd:
                for c in range(4):
                    sp.wait_ge(lo_ready, 4 * rnd + (c - 3))
                    sp.dma_start(raw[:, c, :], w_stream[4 * rnd + c]).then_inc(raw_landed[c], 16)
            for c in range(2):
                sp.wait_ge(lo_ready, DEPTH * CHUNKS + c - 3)
                sp.dma_start(raw[:, c, :], w_stream[c]).then_inc(raw_landed[c], 16)
            sp.wait_ge(x_ready, 2 * DEPTH * NG)
            sp.dma_start(y_out, x[:]).then_inc(stored, 16)
            sp.wait_ge(stored, 16)

        @block.gpsimd
        def _(pool):
            pool.dma_start(consts[:], consts_in).then_inc(small_landed, 16)
            pool.dma_start(par_all[:], params_in).then_inc(small_landed, 16)
            pool.sem_inc(sum_ready, 1)

            def sum_groups(first):
                for n in range(1, NG):
                    pool.wait_ge(squares_ready, first + (n + 1))
                    s = pool.tensor_tensor(slot[:, 0, :], slot[:, 0, :], slot[:, n, :], ALU.add)
                    if n < NG - 1:
                        pool.drain()
                s.then_inc(sum_ready, 1)

            with pool.Fori(0, DEPTH) as l:
                sum_groups(l * 28)
                sum_groups(l * 28 + 4)
                sum_groups(l * 28 + 8)
                with pool.Fori(0, NG) as quarter:
                    sum_groups(l * 28 + quarter * 4 + 12)

        @block.scalar
        def _(act):
            def split(n, c):
                act.wait_ge(chunk_used, n + 1)
                act.activation(w_hi[:, c % 2, :], raw[:, c, :], ACT.Copy).then_inc(hi_ready, 1)

            def round_(l, rnd, tail, mid=None, late=None):
                n = l * CHUNKS + rnd * 4
                use = l * ROUNDS + rnd + 1
                act.wait_ge(raw_landed[2], 16 * use)
                split(n + 2, 2)
                if mid:
                    mid()
                act.wait_ge(raw_landed[3], 16 * use)
                split(n + 3, 3)
                if late:
                    late()
                act.wait_ge(raw_landed[0], 16 * (use + 1))
                split(n + 4, 0)
                act.wait_ge(raw_landed[1], 16 * (use + 1))
                split(n + 5, 1)
                tail()

            def full(l, rnd):
                act.wait_ge(chunk_used, l * CHUNKS + rnd * 4 + (4 + 2))

            def squares(source, n, sums):
                if n == 0:
                    act.wait_ge(sum_ready, sums + 1)
                act.activation(slot[:, n, :], source, ACT.Square).then_inc(squares_ready, 1)

            def group(a, n):
                return a[:, n * GT:(n + 1) * GT, :].rearrange("p i t -> p (i t)")

            def guess_rstd(count):
                act.wait_ge(var_ready, count)
                act.activation(rstd[:], var[:], ACT.Ln)
                act.drain()
                act.activation(rstd[:], rstd[:], ACT.Exp, scale=-0.5).then_inc(rstd_guess, 1)

            def normed_to_hi(done):
                for n in range(NG):
                    act.wait_ge(h_float, done + (n + 1))
                    act.activation(group(h_hi, n), slot[:, 1 + n, :], ACT.Copy).then_inc(h_hi_ready, 1)

            act.wait_ge(x_landed, 16 * NG)
            for c in range(2):
                act.wait_ge(raw_landed[c], 16)
                if c == 0:
                    act.wait_ge(chunk_used, 1)
                act.activation(w_hi[:, c, :], raw[:, c, :], ACT.Copy).then_inc(hi_ready, 1)

            with act.Fori(0, DEPTH) as l:
                for n in range(NG):
                    squares(group(x, n), n, 7 * l)
                guess_rstd(5 * l + 1)
                normed_to_hi(8 * l)

                def glu_gate():
                    full(l, 0)
                    act.activation(factor[:], buf(0), ACT.Sigmoid).then_inc(buf_free[0], 1)
                    act.drain().then_inc(gate_sig, 1)

                round_(l, 0, glu_gate)
                round_(l, 1, lambda: None)
                for i, (dst, half) in enumerate(((q, 0), (k, 0), (q, 1), (k, 1))):
                    def take():
                        full(l, 2 + i)
                        act.activation(group(dst, half), buf(i % 2), ACT.Copy,
                                       scale=SCALE if dst is q else 1.0).then_inc(buf_free[i % 2], 1)
                        act.drain().then_inc(qkv_ready, 1)
                    round_(l, 2 + i, take)

                def scores_to_log(p):
                    act.wait_ge(scores_full, PAIRS * l + (p + 1))
                    act.activation(att[:], scores, ACT.Abs)
                    act.drain()
                    act.activation(att[:], att[:], ACT.Exp, scale=-1.0)
                    act.drain()
                    act.activation(att[:], att[:], ACT.Ln, bias=1.0).then_inc(softplus_log, 1)

                def exponentials(p):
                    act.wait_ge(log_a_ready, PAIRS * l + (p + 1))
                    act.activation(att[:], att[:], ACT.Exp).then_inc(att_ready, 1)

                def heads_out(p):
                    act.wait_ge(out_full, PAIRS * l + (p + 1))
                    act.activation(yb_hi[:, 2 * p:2 * p + 2, :].rearrange("p i t -> p (i t)"), att_out,
                                   ACT.Copy).then_inc(yb_hi_ready, 1)

                def take_v(half):
                    full(l, 6 + half)
                    act.activation(v[:, :, half * 512:(half + 1) * 512], ps[:, 2 * half:2 * half + 2, :],
                                   ACT.Copy).then_inc(buf_free[half], 1)
                    act.drain().then_inc(qkv_ready, 1)

                round_(l, 6, lambda: take_v(0))

                def v1_tail():
                    take_v(1)
                    heads_out(0)

                round_(l, 7, v1_tail, lambda: scores_to_log(0), lambda: exponentials(0))

                def sc_c_tail():
                    full(l, 8)
                    act.activation(factor[:], buf(0), ACT.Copy).then_inc(buf_free[0], 1)
                    act.drain().then_inc(sc_c_ready, 1)
                    heads_out(1)

                def sc_c_mid():
                    scores_to_log(1)
                    act.wait_ge(centred, l + 1)
                    act.activation(ln_work[:], conv_c[:].rearrange("p i t -> p (i t)"),
                                   ACT.Square).then_inc(ln_squared, 1)

                round_(l, 8, sc_c_tail, sc_c_mid, lambda: exponentials(1))

                def sc_u_mid():
                    scores_to_log(2)
                    guess_rstd(5 * l + 2)

                round_(l, 9, lambda: heads_out(2), sc_u_mid, lambda: exponentials(2))

                def sc_b_tail():
                    heads_out(3)
                    act.wait_ge(ln_ready, l + 1)
                    act.activation(ln_work[:], conv_c[:].rearrange("p i t -> p (i t)"),
                                   ACT.Sigmoid).then_inc(ln_sig, 1)
                    act.wait_ge(silu_ready, l + 1)
                    act.activation(group(yc_hi, 0), conv_c[:].rearrange("p i t -> p (i t)"),
                                   ACT.Copy).then_inc(yc_hi_ready, 1)
                    act.wait_ge(ya_float, l + 1)
                    act.activation(group(ya_hi, 0), conv_a[:].rearrange("p i t -> p (i t)"),
                                   ACT.Copy).then_inc(ya_hi_ready, 1)

                round_(l, 10, sc_b_tail, lambda: scores_to_log(3), lambda: exponentials(3))

                with act.Fori(0, NG) as j:
                    for i, b in enumerate((1, 0, 1)):
                        def gate():
                            full(l, j * 4 + (R_HEAD + i))
                            if i == 0:
                                act.wait_ge(gates_free, (NG + 1) * l + j + 1)
                            act.activation(slot[:, i, :], buf(b), ACT.Sigmoid).then_inc(buf_free[b], 1)
                            act.drain().then_inc(gate_ready, 1)
                        round_(l, j * 4 + (R_HEAD + i), gate)

                    def mixed_hi():
                        act.wait_ge(mixed_float, NG * l + j + 1)
                        act.activation(mid_hi[:, bass.ds(j * GT, GT), :], tiles(slot[:, 3, :]),
                                       ACT.Copy).then_inc(mixed_hi_ready, 1)
                    round_(l, j * 4 + (R_HEAD + 3), mixed_hi)

                for n in range(NG):
                    def out_tail():
                        b = (n + 1) % 2
                        full(l, R_HEAD + R_MIX + n)
                        if n == 0:
                            act.wait_ge(gates_free, (NG + 1) * (l + 1))
                        squares(buf(b), n, 7 * l + 1)
                        act.activation(group(y, n), buf(b), ACT.Copy).then_inc(buf_free[b], 1)
                    round_(l, R_HEAD + R_MIX + n, out_tail)

                guess_rstd(5 * l + 3)
                for n in range(NG):
                    act.wait_ge(x_ready, 2 * NG * l + (n + 1))
                    squares(group(x, n), n, 7 * l + 2)
                guess_rstd(5 * l + 4)
                normed_to_hi(8 * l + 4)

                with act.Fori(0, NG) as quarter:
                    first = quarter * (2 * NG) + (R_HEAD + R_MIX + R_OUT)
                    for n in range(NG):
                        def relu():
                            b = (n + 1) % 2
                            full(l, first + n)
                            act.wait_ge(relu_free, l * 16 + quarter * 4 + (n + 1))
                            act.activation(slot[:, 4, :], buf(b), ACT.Relu).then_inc(buf_free[b], 1)
                            act.drain()
                            act.activation(group(mid_hi, n), slot[:, 4, :], ACT.Square).then_inc(f_hi_ready, 1)
                        round_(l, first + n, relu)
                    for n in range(NG):
                        def down():
                            act.wait_ge(y_added, l * 16 + quarter * 4 + (n + 1))
                            squares(group(y, n), n, 7 * l + quarter + 3)
                        round_(l, first + NG + n, down)
                guess_rstd(5 * l + 5)
                act.wait_ge(x_ready, 2 * NG * (l + 1))

        @block.vector
        def _(dve):
            def split(n, c):
                dve.wait_ge(hi_ready, n + 1)
                dve.tensor_tensor(w_lo[:, c % 2, :], raw[:, c, :], w_hi[:, c % 2, :].bitcast(F32),
                                  ALU.subtract).then_inc(lo_ready, 1)

            def round_(l, rnd, tail, mid=None, late=None):
                n = l * CHUNKS + rnd * 4
                split(n + 2, 2)
                if mid:
                    mid()
                split(n + 3, 3)
                if late:
                    late()
                split(n + 4, 0)
                split(n + 5, 1)
                tail()

            def nothing():
                return None

            def full(l, rnd, c=3):
                dve.wait_ge(chunk_used, l * CHUNKS + rnd * 4 + (c + 1 + 2))

            def group(a, n):
                return a[:, n * GT:(n + 1) * GT, :].rearrange("p i t -> p (i t)")

            def flat(a):
                return a[:].rearrange("p i t -> p (i t)")

            def lo(out, exact, hi):
                return dve.tensor_tensor(out, exact, hi.bitcast(F32), ALU.subtract)

            def variance(count, eps):
                dve.wait_ge(stat_full, count)
                dve.tensor_scalar(var[:], stat, eps, None, ALU.add).then_inc(var_ready, 1)

            def refine(count):
                dve.wait_ge(rstd_guess, count)
                dve.scalar_tensor_tensor(newton[:], rstd[:], -0.5, rstd[:], ALU.mult, ALU.mult)
                dve.drain()
                dve.tensor_tensor(newton[:], newton[:], var[:], ALU.mult)
                dve.drain()
                dve.scalar_tensor_tensor(rstd[:], newton[:], 1.5, rstd[:], ALU.add, ALU.mult)
                dve.drain()

            def normed(gain, done):
                for n in range(NG + 1):
                    if n < NG:
                        for i in range(GT):
                            t = n * GT + i
                            s = dve.scalar_tensor_tensor(slot[:, 1 + n, i * T:(i + 1) * T], x[:, t, :],
                                                         par[:, gain + t:gain + t + 1], rstd[:],
                                                         ALU.mult, ALU.mult)
                        s.then_inc(h_float, 1)
                    if n > 0:
                        dve.wait_ge(h_hi_ready, done + n)
                        lo(group(h_lo, n - 1), slot[:, n, :], group(h_hi, n - 1)).then_inc(h_ready, 1)

            def residual(gain):
                for n in range(NG):
                    for i in range(GT):
                        t = n * GT + i
                        dve.scalar_tensor_tensor(slot[:, 4, i * T:(i + 1) * T], y[:, t, :],
                                                 par[:, gain + t:gain + t + 1], rstd[:], ALU.mult, ALU.mult)
                    dve.drain()
                    dve.tensor_tensor(group(x, n), group(x, n), slot[:, 4, :], ALU.add).then_inc(x_ready, 1)
                    dve.drain()

            dve.wait_ge(small_landed, 32)
            dve.wait_ge(x_landed, 16 * NG)
            dve.sem_inc(relu_free, 1)
            split(0, 0)
            split(1, 1)

            with dve.Fori(0, DEPTH) as l:
                dve.tensor_copy(par[:], par_all[:, bass.ds(l * NPAR, NPAR)])
                variance(5 * l + 1, RMS_EPS)
                refine(5 * l + 1)
                normed(G_MIX_PRE, 8 * l)

                taps_done = [0]

                def taps(count):
                    for tap in range(taps_done[0], taps_done[0] + count):
                        for i in range(GT):
                            w = par[:, W_C + i * TAPS_C + tap:W_C + i * TAPS_C + tap + 1]
                            moved = glu_pad[:, i, tap:tap + T]
                            if tap == 0:
                                s = dve.tensor_scalar(conv_c[:, i, :], moved, w, par[:, B_C + i:B_C + i + 1],
                                                      ALU.mult, ALU.add)
                            else:
                                s = dve.scalar_tensor_tensor(conv_c[:, i, :], moved, w, conv_c[:, i, :],
                                                             ALU.mult, ALU.add)
                        if tap < TAPS_C - 1:
                            dve.drain()
                    taps_done[0] += count
                    if count and taps_done[0] == TAPS_C:
                        dve.drain().then_inc(conv_c_ready, 1)

                round_(l, 0, nothing)

                def glu():
                    dve.memset(glu_pad[:, :, 0:PAD_C], 0.0)
                    dve.memset(cu_pad[:, :, 0:PAD_A], 0.0)
                    full(l, 1)
                    dve.wait_ge(gate_sig, l + 1)
                    dve.tensor_tensor(glu_pad[:, :, PAD_C:PAD_C + T], tiles(buf(1)), tiles(factor[:]),
                                      ALU.mult).then_inc(buf_free[1], 1)
                    dve.drain()
                    taps(TAP_PLAN[1][2])

                round_(l, 1, glu)
                for rnd in range(2, 7):
                    early, late, last = TAP_PLAN[rnd]
                    round_(l, rnd, lambda: taps(last), lambda: taps(early), lambda: taps(late))
                assert taps_done[0] == TAPS_C

                def softplus(p):
                    dve.wait_ge(softplus_log, PAIRS * l + (p + 1))
                    for e in range(2):
                        dve.scalar_tensor_tensor(soft[:, e, :], scores[:, e, :], 0.0, att[:, e, :], ALU.max, ALU.add)
                    dve.drain()
                    for e in range(2):
                        for at_ in (0, T):
                            s = dve.tensor_tensor(soft[:, e, at_:at_ + P], soft[:, e, at_:at_ + P],
                                                  consts[:, C_MASK:C_MASK + P], ALU.mult)
                    s.then_inc(softplus_ready, 1)

                def bounded(p):
                    dve.wait_ge(log_a_full, PAIRS * l + (p + 1))
                    dve.tensor_tensor(att[:], scores, consts[:, C_BOUND:C_BOUND + ZW].unsqueeze(1)
                                      .to_broadcast([P, 2, ZW]), ALU.min).then_inc(log_a_ready, 1)

                def heads_lo(p):
                    dve.wait_ge(yb_hi_ready, PAIRS * l + (p + 1))
                    pair = (slice(None), slice(2 * p, 2 * p + 2), slice(None))
                    lo(yb_lo[pair].rearrange("p i t -> p (i t)"), att_out,
                       yb_hi[pair].rearrange("p i t -> p (i t)")).then_inc(yb_ready, 1)

                def v1_tail():
                    heads_lo(0)
                    dve.wait_ge(mean_full, l + 1)
                    dve.tensor_tensor(conv_c[:], conv_c[:], over_tiles(stat), ALU.subtract).then_inc(centred, 1)

                round_(l, 7, v1_tail, lambda: softplus(0), lambda: bounded(0))

                def sc_c_tail():
                    heads_lo(1)
                    variance(5 * l + 2, LN_EPS)

                round_(l, 8, sc_c_tail, lambda: softplus(1), lambda: bounded(1))

                def sc_u_late():
                    bounded(2)
                    refine(5 * l + 2)
                    dve.tensor_tensor(conv_c[:], conv_c[:], over_tiles(rstd[:]), ALU.mult)
                    dve.drain()
                    for i in range(GT):
                        dve.tensor_scalar(conv_c[:, i, :], conv_c[:, i, :], par[:, G_LN + i:G_LN + i + 1],
                                          par[:, B_LN + i:B_LN + i + 1], ALU.mult, ALU.add)
                    dve.drain().then_inc(ln_ready, 1)

                def sc_u_tail():
                    full(l, 9)
                    dve.wait_ge(sc_c_ready, l + 1)
                    dve.tensor_tensor(cu_pad[:, :, PAD_A:PAD_A + T], tiles(buf(1)), tiles(factor[:]),
                                      ALU.mult).then_inc(buf_free[1], 1)
                    dve.drain()
                    heads_lo(2)

                round_(l, 9, sc_u_tail, lambda: softplus(2), sc_u_late)

                def sc_b_mid():
                    softplus(3)
                    for tap in range(TAPS_A):
                        for i in range(GT):
                            w = par[:, W_A + i * TAPS_A + tap:W_A + i * TAPS_A + tap + 1]
                            moved = cu_pad[:, i, tap:tap + T]
                            if tap == 0:
                                dve.tensor_scalar(conv_a[:, i, :], moved, w, None, ALU.mult)
                            else:
                                dve.scalar_tensor_tensor(conv_a[:, i, :], moved, w, conv_a[:, i, :],
                                                         ALU.mult, ALU.add)
                        dve.drain()

                def sc_b_tail():
                    heads_lo(3)
                    dve.wait_ge(ln_sig, l + 1)
                    dve.tensor_tensor(flat(conv_c), flat(conv_c), ln_work[:], ALU.mult).then_inc(silu_ready, 1)
                    full(l, 10)
                    dve.tensor_tensor(flat(conv_a), buf(0), flat(conv_a), ALU.mult).then_inc(buf_free[0], 1)
                    dve.drain().then_inc(ya_float, 1)
                    dve.wait_ge(yc_hi_ready, l + 1)
                    lo(group(yc_lo, 0), flat(conv_c), group(yc_hi, 0)).then_inc(yc_ready, 1)
                    dve.wait_ge(ya_hi_ready, l + 1)
                    lo(group(ya_lo, 0), flat(conv_a), group(ya_hi, 0)).then_inc(ya_ready, 1)
                    dve.drain().then_inc(gates_free, 1)

                round_(l, 10, sc_b_tail, sc_b_mid, lambda: bounded(3))

                with dve.Fori(0, NG) as j:
                    for i in range(3):
                        round_(l, j * 4 + (R_HEAD + i), nothing)

                    def branch_a():
                        dve.wait_ge(gate_ready, 3 * NG * l + j * 3 + 3)
                        full(l, j * 4 + (R_HEAD + 3), 0)
                        dve.tensor_tensor(slot[:, 3, :], buf(0), slot[:, 0, :], ALU.mult).then_inc(buf_free[0], 1)
                        dve.drain()

                    def branch_c():
                        full(l, j * 4 + (R_HEAD + 3), 1)
                        dve.tensor_tensor(slot[:, 4, :], buf(2), slot[:, 2, :], ALU.mult)
                        dve.drain()
                        dve.tensor_tensor(slot[:, 3, :], slot[:, 3, :], slot[:, 4, :], ALU.add)
                        dve.drain()

                    def branch_b():
                        full(l, j * 4 + (R_HEAD + 3))
                        dve.tensor_tensor(slot[:, 4, :], buf(3), slot[:, 1, :], ALU.mult)
                        dve.drain()
                        dve.tensor_tensor(slot[:, 3, :], slot[:, 3, :], slot[:, 4, :], ALU.add)
                        dve.drain().then_inc(mixed_float, 1)
                        dve.wait_ge(mixed_hi_ready, NG * l + j + 1)
                        lo(mid_lo[:, bass.ds(j * GT, GT), :], tiles(slot[:, 3, :]),
                           mid_hi[:, bass.ds(j * GT, GT), :]).then_inc(mixed_ready, 1)
                        dve.drain().then_inc(gates_free, 1)

                    round_(l, j * 4 + (R_HEAD + 3), branch_b, branch_a, branch_c)

                with dve.Fori(0, NG) as n:
                    round_(l, n + (R_HEAD + R_MIX), nothing)
                variance(5 * l + 3, RMS_EPS)
                refine(5 * l + 3)
                residual(G_MIX_POST)
                variance(5 * l + 4, RMS_EPS)
                refine(5 * l + 4)
                normed(G_MLP_PRE, 8 * l + 4)
                dve.memset(y[:], 0.0)
                dve.drain()

                with dve.Fori(0, NG) as quarter:
                    first = quarter * (2 * NG) + (R_HEAD + R_MIX + R_OUT)
                    for n in range(NG):
                        def squared_relu():
                            done = l * 16 + quarter * 4 + (n + 1)
                            dve.wait_ge(f_hi_ready, done)
                            dve.tensor_tensor(slot[:, 4, :], slot[:, 4, :], slot[:, 4, :], ALU.mult)
                            dve.drain()
                            lo(group(mid_lo, n), slot[:, 4, :], group(mid_hi, n)).then_inc(f_ready, 1)
                            dve.drain().then_inc(relu_free, 1)
                        round_(l, first + n, squared_relu)
                    for n in range(NG):
                        def down():
                            b = (n + 1) % 2
                            full(l, first + NG + n)
                            dve.tensor_tensor(group(y, n), group(y, n), buf(b), ALU.add).then_inc(buf_free[b], 1)
                            dve.drain().then_inc(y_added, 1)
                        round_(l, first + NG + n, down)

                variance(5 * l + 5, RMS_EPS)
                refine(5 * l + 5)
                residual(G_MLP_POST)

        @block.tensor
        def _(pe):
            pe.sem_inc(chunk_used, 2)
            pe.sem_inc(buf_free[0], 1)
            pe.sem_inc(buf_free[1], 1)

            def chunk(n, c, out, hi, lo, tile0, first, last):
                pe.wait_ge(lo_ready, n + 1)
                for kk in range(KK):
                    for i in range(GT):
                        w = (slice(None), c % 2, slice((kk * GT + i) * P, (kk * GT + i + 1) * P))
                        o = out[:, i * T:(i + 1) * T]
                        t = tile0 + kk
                        pe.matmul(o, w_hi[w], hi[:, t, :], start=first and kk == 0 and i % 2 == 0, stop=False,
                                  skip_group_check=True)
                        pe.matmul(o, w_hi[w], lo[:, t, :], start=False, stop=False, skip_group_check=True)
                        s = pe.matmul(o, w_lo[w], hi[:, t, :], start=False, stop=last and kk == KK - 1,
                                      skip_group_check=True)
                s.then_inc(chunk_used, 1)

            def round_(l, rnd, b, use, hi, lo, ready=None, between=None):
                pe.wait_ge(buf_free[b], l * USES[b] + use + 1)
                n = l * CHUNKS + rnd * 4
                for c in range(4):
                    if ready:
                        pe.wait_ge(ready[0], ready[1] + (c + 1))
                    chunk(n + c, c, buf(b), hi, lo, c * KK, c == 0, c == 3)
                    if between:
                        between(c)

            def statistics(ones, source, done):
                for i in range(GT):
                    s = pe.matmul(stat, consts[:, ones:ones + P], source[:, i * T:(i + 1) * T],
                                  start=i == 0, stop=i == GT - 1)
                s.then_inc(done, 1)

            def norm(l, sums):
                pe.wait_ge(sum_ready, 7 * l + (sums + 1))
                statistics(C_RMS, slot[:, 0, :], stat_full)

            pe.wait_ge(small_landed, 32)
            with pe.Fori(0, DEPTH) as l:
                norm(l, 1)
                with pe.Fori(0, 3) as i:
                    for b in range(2):
                        round_(l, i * 2 + b, b, i, h_hi, h_lo, (h_ready, 8 * l))

                def attention(c, p):
                    if c == 0:
                        pe.wait_ge(qkv_ready, 6 * l + 4)
                        for e in range(2):
                            hd = 2 * p + e
                            pe.matmul(scores[:, e, 0:T], k[:, hd, 0:P], q[:, hd, :], start=True, stop=False,
                                      skip_group_check=True)
                            s = pe.matmul(scores[:, e, T:ZW], k[:, hd, P:T], q[:, hd, P:T], start=False,
                                          stop=False, skip_group_check=True)
                        s.then_inc(scores_full, 1)
                    if c == 1:
                        pe.wait_ge(softplus_ready, PAIRS * l + (p + 1))
                        for e in range(2):
                            up_to, all_ = consts[:, C_NU:C_NU + P], consts[:, C_NO:C_NO + P]
                            pe.matmul(scores[:, e, 0:T], up_to, soft[:, e, 0:T], start=False, stop=False,
                                      skip_group_check=True)
                            pe.matmul(scores[:, e, P:T], all_, soft[:, e, T:ZW], start=False, stop=True,
                                      skip_group_check=True)
                            s = pe.matmul(scores[:, e, T:ZW], up_to, soft[:, e, T:ZW], start=False, stop=True,
                                          skip_group_check=True)
                        s.then_inc(log_a_full, 1)
                    if c == 2:
                        pe.wait_ge(att_ready, PAIRS * l + (p + 1))
                        pe.wait_ge(qkv_ready, 6 * l + (5 if p < PAIRS // 2 else 6))
                        if p:
                            pe.wait_ge(yb_ready, PAIRS * l + p)
                        for e in range(2):
                            hd = 2 * p + e
                            pe.matmul(att_out[:, e * T:(e + 1) * T], v[:, 0, hd * HD:(hd + 1) * HD],
                                      att[:, e, 0:T], start=True, stop=False, skip_group_check=True)
                            s = pe.matmul(att_out[:, e * T + P:(e + 1) * T], v[:, 1, hd * HD:(hd + 1) * HD],
                                          att[:, e, T:ZW], start=False, stop=True, skip_group_check=True)
                        s.then_inc(out_full, 1)

                for half in range(2):
                    pe.wait_ge(buf_free[half], l * USES[half] + 4)
                    for c in range(4):
                        n = l * CHUNKS + (6 + half) * 4 + c
                        pe.wait_ge(lo_ready, n + 1)
                        for kk in range(KK):
                            w = (slice(None), c % 2, slice(kk * GT * P, (kk + 1) * GT * P))
                            for t in range(2):
                                h = (slice(None), c * KK + kk, slice(t * P, (t + 1) * P))
                                o = ps[:, 2 * half + t, :]
                                pe.matmul(o, h_hi[h], w_hi[w], start=c == 0 and kk == 0, stop=False,
                                          skip_group_check=True)
                                pe.matmul(o, h_hi[h], w_lo[w], start=False, stop=False, skip_group_check=True)
                                s = pe.matmul(o, h_lo[h], w_hi[w], start=False, stop=c == 3 and kk == KK - 1,
                                              skip_group_check=True)
                        s.then_inc(chunk_used, 1)
                        if half == 1:
                            attention(c, 0)
                            if c == 3:
                                pe.wait_ge(conv_c_ready, l + 1)
                                statistics(C_LN, conv_c[:].rearrange("p i t -> p (i t)"), mean_full)

                def beside_sc_c(c):
                    attention(c, 1)
                    if c == 3:
                        pe.wait_ge(ln_squared, l + 1)
                        statistics(C_LN, ln_work, stat_full)

                round_(l, 8, 0, 4, h_hi, h_lo, between=beside_sc_c)
                round_(l, 9, 1, 4, h_hi, h_lo, between=lambda c: attention(c, 2))
                round_(l, 10, 0, 5, h_hi, h_lo, between=lambda c: attention(c, 3))

                with pe.Fori(0, NG) as j:
                    for i, b in enumerate((1, 0, 1)):
                        round_(l, j * 4 + (R_HEAD + i), b, j * 2 + ((6, 5)[b] + i // 2), h_hi, h_lo)
                    n = l * CHUNKS + j * 16 + (4 * (R_HEAD + 3))
                    pe.wait_ge(ya_ready, l + 1)
                    pe.wait_ge(buf_free[0], l * USES[0] + j * 2 + 8)
                    chunk(n, 0, buf(0), ya_hi, ya_lo, 0, True, True)
                    pe.wait_ge(gates_free, (NG + 1) * l + j + 1)
                    chunk(n + 1, 1, buf(2), yc_hi, yc_lo, 0, True, True)
                    for c in range(2):
                        chunk(n + (2 + c), 2 + c, buf(3), yb_hi, yb_lo, c * KK, c == 0, c == 1)

                with pe.Fori(0, 2) as i:
                    for e, b in enumerate((1, 0)):
                        round_(l, i * 2 + (R_HEAD + R_MIX + e), b, i + (14, 13)[b], mid_hi, mid_lo,
                               (mixed_ready, NG * l))
                norm(l, 2)
                norm(l, 3)

                with pe.Fori(0, NG) as quarter:
                    first = quarter * (2 * NG) + (R_HEAD + R_MIX + R_OUT)
                    with pe.Fori(0, 2) as i:
                        for e, b in enumerate((1, 0)):
                            round_(l, first + i * 2 + e, b, quarter * 4 + i + (16, 15)[b], h_hi, h_lo,
                                   (h_ready, 8 * l + 4))
                    with pe.Fori(0, 2) as i:
                        for e, b in enumerate((1, 0)):
                            round_(l, first + i * 2 + (NG + e), b, quarter * 4 + i + (18, 17)[b], mid_hi, mid_lo,
                                   (f_ready, l * 16 + quarter * 4))
                norm(l, 7)


def constants():
    s, t = np.arange(P)[:, None], np.arange(P)[None, :]
    c = np.zeros((P, NCONST), np.float32)
    c[:, C_RMS:C_RMS + P] = 1.0 / D
    c[:, C_LN:C_LN + P] = 1.0 / D_CF
    c[:, C_NU:C_NU + P] = np.where(s >= t, -1.0, 0.0)
    c[:, C_NO:C_NO + P] = -1.0
    c[:, C_MASK:C_MASK + P] = np.where(s < t, 1.0, 0.0)
    c[:, C_BOUND:C_BOUND + ZW] = BIG
    for at in (0, T):
        c[:, C_BOUND + at:C_BOUND + at + P] = np.where(s < t, BIG, -BIG)
    return c


def chunks(w):
    kdim, n = w.shape
    return w.reshape(kdim // (KK * P), KK, P, n // (GT * P), GT * P).transpose(3, 0, 2, 1, 4)


def weight_stream(w_in, proj_a, proj_b, proj_c, w_o, w_up, w_down):
    stream = np.empty((DEPTH * CHUNKS, P, KK, GT * P), np.float32)
    at = 0

    def put(c):
        nonlocal at
        stream[at:at + c.shape[0]] = c
        at += c.shape[0]

    sc = 3 * D_ATT // (GT * P)
    glu, gates = sc + 3 * D_SC // (GT * P), sc + (3 * D_SC + 2 * D_CF) // (GT * P)
    for l in range(DEPTH):
        win = chunks(w_in[l])
        for g in (glu + 1, glu, 0, 2, 1, 3, 4, 5, sc + 1, sc + 2, sc):
            put(win[g])
        pa, pb, pc = chunks(proj_a[l]), chunks(proj_b[l]), chunks(proj_c[l])
        for j in range(NG):
            for branch in range(3):
                put(win[gates + branch * NG + j])
            put(pa[j])
            put(pc[j])
            put(pb[j])
        for g in chunks(w_o[l]):
            put(g)
        up, down = chunks(w_up[l]), chunks(w_down[l])
        for quarter in range(NG):
            for n in range(NG):
                put(up[quarter * NG + n])
            for n in range(NG):
                put(down[n, quarter * NG:(quarter + 1) * NG])
    assert at == DEPTH * CHUNKS
    return stream.reshape(DEPTH * CHUNKS, P, CW)


def by_partition(a):
    a = np.asarray(a)
    return np.moveaxis(a.reshape(*a.shape[:-1], a.shape[-1] // P, P), -1, 0)


def kernel(x, ln_mix_pre, ln_mix_post, ln_mlp_pre, ln_mlp_post, w_in, conv_a_w, proj_a, proj_b, conv_c_w,
           conv_c_b, norm_c_g, norm_c_b, proj_c, w_o, w_up, w_down):
    import concourse.bacc as bacc
    from concourse.bass_utils import run_bass_kernel_spmd

    params = np.empty((P, DEPTH, NPAR), np.float32)
    for at, a in ((G_MIX_PRE, ln_mix_pre), (G_MIX_POST, ln_mix_post), (G_MLP_PRE, ln_mlp_pre),
                  (G_MLP_POST, ln_mlp_post), (B_C, conv_c_b), (G_LN, norm_c_g), (B_LN, norm_c_b)):
        a = by_partition(a)
        params[:, :, at:at + a.shape[-1]] = a
    for at, a in ((W_A, conv_a_w), (W_C, conv_c_w)):
        a = by_partition(a)
        params[:, :, at:at + a.shape[2] * a.shape[3]] = a.transpose(0, 1, 3, 2).reshape(P, DEPTH, -1)
    arrays = {
        "w_stream": weight_stream(*(np.asarray(a) for a in (w_in, proj_a, proj_b, proj_c, w_o, w_up, w_down))),
        "x_in": np.ascontiguousarray(by_partition(np.asarray(x)[0]).transpose(0, 2, 1)),
        "params_in": params.reshape(P, DEPTH * NPAR),
        "consts_in": constants(),
    }
    nc = bacc.Bacc("TRN2", target_bir_lowering=False, num_devices=1)
    args = [nc.dram_tensor(name, a.shape, F32, kind="ExternalInput").ap() for name, a in arrays.items()]
    y_out = nc.dram_tensor("y_out", (P, NT, T), F32, kind="ExternalOutput").ap()
    build(nc, *args, y_out)
    result = run_bass_kernel_spmd(nc, [arrays], core_ids=[0]).results[0]["y_out"]
    return result.transpose(2, 1, 0).reshape(1, T, D)
```

```python
from contextlib import ExitStack

import numpy as np

import concourse.bass as bass
import concourse.mybir as mybir

F32 = mybir.dt.float32
F32R = mybir.dt.float32r
ALU = mybir.AluOpType
ACT = mybir.ActivationFunctionType

P = 128
T = 256
D = 2048
DEPTH = 2
HEADS, HD = 8, 128
D_ATT, D_SC, D_CF, D_FF = D // 2, D // 4, D // 4, 4 * D
TAPS_A, TAPS_C = 3, 31
RMS_EPS, LN_EPS = 1e-6, 1e-5
SCALE = HD ** -0.5
NT = D // P
GT = 4
NG = NT // GT
X_HALVES = 2 * (NG - 1)
GW = GT * T
KK = 4
CW = KK * GT * P
PAIRS = HEADS // 2
ZW = T + P
BIG = 3e38

G_MIX_PRE, G_MIX_POST, G_MLP_PRE = 0, NT, 2 * NT
W_A = 3 * NT
W_C = W_A + GT * TAPS_A
B_C = W_C + GT * TAPS_C
G_LN = B_C + GT
B_LN = G_LN + GT
G_MLP_POST = B_LN + GT
NPAR = G_MLP_POST + NT

C_RMS, C_LN, C_NU, C_NO, C_MASK, C_BOUND = 0, P, 2 * P, 3 * P, 4 * P, 5 * P
C_RMS_EPS, C_LN_EPS = C_BOUND + ZW, C_BOUND + ZW + 1
NCONST = C_BOUND + ZW + 2

R_HEAD = 11
R_MIX = 4 * NG
R_OUT = NG
R_MLP = 2 * NG * NG
ROUNDS = R_HEAD + R_MIX + R_OUT + R_MLP
CHUNKS = 4 * ROUNDS
HALVES = 2 * CHUNKS
HALF = CW // 2
AHEAD = 3
USES = (32, 31)
TAP_PLAN = {1: (0, 0, 2), 2: (2, 2, 1), 3: (2, 2, 1), 4: (2, 2, 1), 5: (2, 2, 1), 6: (2, 2, 1), 7: (0, 2, 2)}


def build(nc, w_stream, x_in, params_in, consts_in, y_out):
    ctx = ExitStack()
    with ctx:
        def sem(name):
            return ctx.enter_context(nc.semaphore(name))

        KB = 1024
        slab = ctx.enter_context(nc.sbuf_tensor("slab", [P, 207 * KB // 4], F32))
        base = nc.lookup_mloc(slab).addr
        taken = [0]

        def region(size):
            at = taken[0]
            taken[0] += -(-size // 32) * 32
            assert taken[0] <= 207 * KB
            return at

        def at(name, shape, dt, offset):
            return nc.alloc_sbuf_tensor_at(name, shape, dt, offset=base + offset)

        raw = at("raw", [P, 4, CW], F32, region(32 * KB))
        w_hi = at("w_hi", [P, 4, HALF], F32R, region(16 * KB))
        w_lo = at("w_lo", [P, 4, HALF], F32R, region(16 * KB))
        x = at("x_res", [P, NT, T], F32, region(16 * KB))
        h_hi = at("h_hi", [P, NT, T], F32R, region(16 * KB))
        h_lo = at("h_lo", [P, NT, T], F32R, region(16 * KB))

        m = region(32 * KB)
        mid_hi = at("mid_hi", [P, NT, T], F32R, m)
        mid_lo = at("mid_lo", [P, NT, T], F32R, m + 16 * KB)
        q = at("q", [P, HEADS, T], F32, m)
        k = at("k", [P, HEADS, T], F32, m + 8 * KB)
        v = at("v", [P, 2, D_ATT], F32, m + 16 * KB)
        att = at("att", [P, 2, ZW], F32, m + 24 * KB)
        soft = at("soft", [P, 2, ZW], F32, m + 27 * KB)

        r = region(32 * KB)
        ya_hi = at("ya_hi", [P, GT, T], F32R, r)
        ya_lo = at("ya_lo", [P, GT, T], F32R, r + 4 * KB)
        yc_hi = at("yc_hi", [P, GT, T], F32R, r + 8 * KB)
        yc_lo = at("yc_lo", [P, GT, T], F32R, r + 12 * KB)
        yb_hi = at("yb_hi", [P, HEADS, T], F32R, r + 16 * KB)
        yb_lo = at("yb_lo", [P, HEADS, T], F32R, r + 24 * KB)
        y = at("y_sub", [P, NT, T], F32, r)
        factor = at("factor", [P, GW], F32, r)
        ln_work = at("ln_work", [P, GW], F32, r + 4 * KB)

        g = region(20 * KB)
        slot = at("slot", [P, 5, GW], F32, g)
        PAD_C, PAD_A = TAPS_C - 1, TAPS_A - 1
        glu_pad = at("glu_pad", [P, GT, PAD_C + T], F32, g)
        conv_c = at("conv_c", [P, GT, T], F32, g + 4608)
        cu_pad = at("cu_pad", [P, GT, PAD_A + T], F32, g + 8704)
        conv_a = at("conv_a", [P, GT, T], F32, g + 12864)

        TV = T + 2
        var = at("var", [P, TV], F32, region(4 * TV))
        rstd = at("rstd", [P, TV], F32, region(4 * TV))
        newton = at("newton", [P, TV], F32, region(4 * TV))
        consts = at("consts", [P, NCONST], F32, region(4 * NCONST))
        par_all = at("par_all", [P, (DEPTH + 1) * NPAR], F32, region(4 * (DEPTH + 1) * NPAR))
        par = at("par", [P, NPAR], F32, region(4 * NPAR))

        ps = ctx.enter_context(nc.psum_tensor("ps", [P, 8, 512], F32))

        def buf(b):
            return ps[:, 2 * b:2 * b + 2, :].rearrange("p b c -> p (b c)")

        scores = ps[:, 4:6, 0:ZW]
        att_out = ps[:, 6, :]
        stat = ps[:, 7, 0:TV]

        def tiles(ap):
            return ap.rearrange("p (i t) -> p i t", t=T)

        def over_tiles(ap):
            return ap.unsqueeze(1).to_broadcast([P, GT, T])

        first_half_landed = sem("first_half_landed")
        raw_landed = [sem(f"raw_landed{c}") for c in range(4)]
        x_landed = [sem(f"x_landed{n}") for n in range(NG)]
        consts_landed = sem("consts_landed")
        params_landed = sem("params_landed")
        hi_ready = sem("hi_ready")
        lo_ready = sem("lo_ready")
        half_used = sem("half_used")
        buf_free = [sem("buf0_free"), sem("buf1_free")]
        par_ready = sem("par_ready")
        squares_ready = sem("squares_ready")
        sum_ready = sem("sum_ready")
        stat_full = sem("stat_full")
        stat_logged = sem("stat_logged")
        rstd_guess = sem("rstd_guess")
        rstd_ready = sem("rstd_ready")
        y_scaled = sem("y_scaled")
        h_hi_ready = sem("h_hi_ready")
        h_ready = sem("h_ready")
        x_ready = sem("x_ready")
        x_last_ready = sem("x_last_ready")
        glu_scaled = sem("glu_scaled")
        gate_sig = sem("gate_sig")
        qk_ready = sem("qk_ready")
        v_ready = sem("v_ready")
        conv_c_ready = sem("conv_c_ready")
        mean_full = sem("mean_full")
        centred = sem("centred")
        ln_squared = sem("ln_squared")
        ln_ready = sem("ln_ready")
        ln_sig = sem("ln_sig")
        silu_ready = sem("silu_ready")
        yc_hi_ready = sem("yc_hi_ready")
        ya_float = sem("ya_float")
        ya_hi_ready = sem("ya_hi_ready")
        ya_ready = sem("ya_ready")
        scores_full = sem("scores_full")
        softplus_log = sem("softplus_log")
        softplus_ready = sem("softplus_ready")
        log_a_full = sem("log_a_full")
        log_a_ready = sem("log_a_ready")
        att_ready = sem("att_ready")
        out_full = sem("out_full")
        yb_hi_ready = sem("yb_hi_ready")
        yb_ready = sem("yb_ready")
        gate_scaled = sem("gate_scaled")
        gate_ready = sem("gate_ready")
        proj_free = sem("proj_free")
        mixed_float = sem("mixed_float")
        mixed_hi_ready = sem("mixed_hi_ready")
        mixed_ready = sem("mixed_ready")
        y_added = sem("y_added")
        f_float = sem("f_float")
        y_gained = sem("y_gained")
        f_hi_ready = sem("f_hi_ready")
        f_ready = sem("f_ready")
        stored = sem("stored")

        block = ctx.enter_context(nc.Block())

        @block.sync
        def _(sp):
            def load_x(n):
                group = (slice(None), slice(n * GT, (n + 1) * GT), slice(None))
                sp.dma_start(x[group], x_in[group]).then_inc(x_landed[n], 16)

            def load_first(c):
                sp.dma_start(raw[:, c, :], w_stream[c]).then_inc(raw_landed[c], 16)

            load_x(0)
            sp.dma_start(raw[:, 0, 0:HALF], w_stream[0, :, 0:HALF]).then_inc(first_half_landed, 16)
            sp.dma_start(raw[:, 0, HALF:CW], w_stream[0, :, HALF:CW]).then_inc(raw_landed[0], 16)
            load_first(1)
            load_x(1)
            sp.dma_start(consts[:], consts_in).then_inc(consts_landed, 16)
            for c in (2, 3):
                load_x(c)
                load_first(c)
            with sp.Fori(1, DEPTH * ROUNDS) as rnd:
                for c in range(4):
                    sp.wait_ge(lo_ready, 8 * rnd + 2 * (c - 3))
                    sp.dma_start(raw[:, c, :], w_stream[4 * rnd + c]).then_inc(raw_landed[c], 16)
            for c in range(2):
                sp.wait_ge(lo_ready, DEPTH * HALVES + 2 * (c - 3))
                sp.dma_start(raw[:, c, :], w_stream[c]).then_inc(raw_landed[c], 16)
            for c in range(NG):
                if c < NG - 1:
                    sp.wait_ge(x_ready, 2 * DEPTH * X_HALVES + 2 * (c + 1))
                else:
                    sp.wait_ge(x_last_ready, 2 * DEPTH + 1)
                group = (slice(None), slice(c * GT, (c + 1) * GT), slice(None))
                sp.dma_start(y_out[group], x[group]).then_inc(stored, 16)
            sp.wait_ge(stored, 16 * NG)

        @block.gpsimd
        def _(pool):
            pool.sem_inc(sum_ready, 1)
            pool.sem_inc(x_last_ready, 1)

            def sum_groups(first, groups=NG):
                for n in range(1, groups):
                    pool.wait_ge(squares_ready, first + (n + 1))
                    s = pool.tensor_tensor(slot[:, 0, :], slot[:, 0, :], slot[:, n, :], ALU.add)
                    if n < groups - 1:
                        pool.drain()
                s.then_inc(sum_ready, 1)

            def scale_y(n):
                ys = y[:, n * GT:(n + 1) * GT, :]
                pool.tensor_tensor(ys, ys, rstd[:, 0:T].unsqueeze(1).to_broadcast([P, GT, T]),
                                   ALU.mult).then_inc(y_scaled, 1)

            with pool.Fori(0, DEPTH) as l:
                sum_groups(l * 28)
                sum_groups(l * 28 + 4, NG - 1)
                pool.wait_ge(rstd_ready, 2 * l + 1)
                pool.wait_ge(buf_free[0], l * USES[0] + 17)
                for n in range(1, NG):
                    scale_y(n)
                pool.drain()
                last = (slice(None), slice((NG - 1) * GT, NT), slice(None))
                pool.tensor_tensor(x[last], x[last], y[last], ALU.add).then_inc(x_last_ready, 1)
                sum_groups(l * 28 + 8)
                with pool.Fori(0, NG) as quarter:
                    sum_groups(l * 28 + quarter * 4 + 12, NG - 1)
                pool.wait_ge(rstd_ready, 2 * l + 2)
                for n in range(1, NG):
                    pool.wait_ge(y_gained, NG * l + (n + 1))
                    scale_y(n)

        @block.scalar
        def _(act):
            def split(l, rnd, m, landed=None):
                if landed:
                    act.wait_ge(landed, 16)
                elif m % 2 == 0:
                    act.wait_ge(raw_landed[m // 2], 16 * (l * ROUNDS + rnd + 1))
                act.wait_ge(half_used, l * HALVES + rnd * 8 + (m + 1))
                act.activation(w_hi[:, m % 4, :], raw[:, m // 2, m % 2 * HALF:(m % 2 + 1) * HALF],
                               ACT.Copy).then_inc(hi_ready, 1)

            def round_(l, rnd, tail, hooks={}):
                for m in range(8):
                    if m in hooks:
                        hooks[m]()
                    ahead = m + AHEAD
                    split(l, rnd + ahead // 8, ahead % 8)
                tail()

            def full(l, rnd):
                act.wait_ge(half_used, l * HALVES + rnd * 8 + (8 + 4))

            def squares(source, n, sums):
                if n == 0:
                    act.wait_ge(sum_ready, sums + 1)
                act.activation(slot[:, n, :], source, ACT.Square).then_inc(squares_ready, 1)

            def group(a, n):
                return a[:, n * GT:(n + 1) * GT, :].rearrange("p i t -> p (i t)")

            def guess_rstd(count, r=rstd[:], w=TV, eps=C_RMS_EPS):
                act.wait_ge(stat_full, count)
                act.activation(r, stat[:, 0:w], ACT.Ln, bias=consts[:, eps:eps + 1]).then_inc(stat_logged, 1)
                act.drain()
                act.activation(r, r, ACT.Exp, scale=-0.5).then_inc(rstd_guess, 1)

            def gained(n, gain, norm, halves=(0, 1)):
                act.wait_ge(x_landed[n], 16)
                for half in halves:
                    if n < NG - 1:
                        act.wait_ge(x_ready, norm * X_HALVES + (2 * n + half + 1))
                    else:
                        act.wait_ge(x_last_ready, norm + 1)
                    for i in range(2):
                        t = n * GT + 2 * half + i
                        s = act.activation(h_hi[:, t, :], x[:, t, :], ACT.Copy, scale=par[:, gain + t:gain + t + 1])
                    s.then_inc(h_hi_ready, 1)

            def ln_and_exp():
                act.preload_act_table_set("natural_log_exp_and_others")

            act.dma_start(par_all[:], params_in).then_inc(params_landed, 16)
            ln_and_exp()
            act.wait_ge(par_ready, 1)
            gained(0, G_MIX_PRE, 0, (0,))
            split(0, 0, 0, first_half_landed)
            gained(0, G_MIX_PRE, 0, (1,))
            split(0, 0, 1, raw_landed[0])
            split(0, 0, 2)
            act.wait_ge(consts_landed, 16)

            with act.Fori(0, DEPTH) as l:
                def input_hooks(gain, sums, norm):
                    def squares_of(*members):
                        for n in members:
                            squares(group(x, n), n, sums)
                    return {0: lambda: gained(1, gain, norm), 1: lambda: gained(2, gain, norm),
                            3: lambda: gained(3, gain, norm), 4: lambda: squares_of(0, 1),
                            5: lambda: squares_of(2), 6: lambda: squares_of(3)}

                def glu_gate():
                    act.wait_ge(glu_scaled, l + 1)
                    act.activation(factor[:], factor[:], ACT.Sigmoid).then_inc(gate_sig, 1)

                def nothing():
                    return None

                round_(l, 0, nothing, input_hooks(G_MIX_PRE, 7 * l, 2 * l))
                round_(l, 1, nothing, {3: lambda: guess_rstd(5 * l + 1), 5: glu_gate})
                with act.Fori(2, 6) as rnd:
                    round_(l, rnd, nothing)

                def scores_to_log(p):
                    act.wait_ge(scores_full, PAIRS * l + (p + 1))
                    act.activation(att[:], scores, ACT.Abs)
                    act.drain()
                    act.activation(att[:], att[:], ACT.Exp, scale=-1.0)
                    act.drain()
                    act.activation(att[:], att[:], ACT.Ln, bias=1.0).then_inc(softplus_log, 1)

                def exponentials(p):
                    act.wait_ge(log_a_ready, PAIRS * l + (p + 1))
                    act.activation(att[:], att[:], ACT.Exp).then_inc(att_ready, 1)

                def heads_out(p):
                    act.wait_ge(out_full, PAIRS * l + (p + 1))
                    act.activation(yb_hi[:, 2 * p:2 * p + 2, :].rearrange("p i t -> p (i t)"), att_out,
                                   ACT.Copy).then_inc(yb_hi_ready, 1)

                def take_v(half):
                    full(l, 6 + half)
                    for t in range(2):
                        s = act.activation(v[:, t, half * 512:(half + 1) * 512], ps[:, 2 * half + t, :], ACT.Copy,
                                           scale=rstd[:, T + t:T + t + 1])
                    s.then_inc(buf_free[half], 1)
                    act.drain().then_inc(v_ready, 1)

                round_(l, 6, lambda: (take_v(0), ln_and_exp()))

                def v1_tail():
                    take_v(1)
                    heads_out(0)

                round_(l, 7, v1_tail, {3: lambda: scores_to_log(0), 5: lambda: exponentials(0)})

                def sc_c_tail():
                    heads_out(1)
                    act.wait_ge(centred, l + 1)
                    act.activation(ln_work[:], conv_c[:].rearrange("p i t -> p (i t)"),
                                   ACT.Square).then_inc(ln_squared, 1)

                round_(l, 8, sc_c_tail, {3: lambda: scores_to_log(1), 5: lambda: exponentials(1)})

                def sc_u_late():
                    exponentials(2)
                    guess_rstd(5 * l + 2, ln_work[:, 0:T], T, C_LN_EPS)

                round_(l, 9, lambda: heads_out(2), {3: lambda: scores_to_log(2), 5: sc_u_late})

                def ln_sigmoid():
                    act.wait_ge(ln_ready, l + 1)
                    act.activation(ln_work[:], conv_c[:].rearrange("p i t -> p (i t)"),
                                   ACT.Sigmoid).then_inc(ln_sig, 1)

                def sc_b_tail():
                    heads_out(3)
                    act.wait_ge(silu_ready, l + 1)
                    act.activation(group(yc_hi, 0), conv_c[:].rearrange("p i t -> p (i t)"),
                                   ACT.Copy).then_inc(yc_hi_ready, 1)
                    act.wait_ge(ya_float, l + 1)
                    act.activation(group(ya_hi, 0), conv_a[:].rearrange("p i t -> p (i t)"),
                                   ACT.Copy).then_inc(ya_hi_ready, 1)

                round_(l, 10, sc_b_tail, {3: lambda: scores_to_log(3), 5: lambda: exponentials(3), 6: ln_sigmoid})

                with act.Fori(0, NG) as j:
                    for i in range(3):
                        def gate():
                            act.wait_ge(gate_scaled, 3 * NG * l + j * 3 + (i + 1))
                            act.activation(slot[:, i, :], slot[:, i, :], ACT.Sigmoid).then_inc(gate_ready, 1)
                        round_(l, j * 4 + (R_HEAD + i), gate)

                    def mixed_hi():
                        act.wait_ge(mixed_float, NG * l + j + 1)
                        act.activation(mid_hi[:, bass.ds(j * GT, GT), :], tiles(slot[:, 3, :]),
                                       ACT.Copy).then_inc(mixed_hi_ready, 1)
                    round_(l, j * 4 + (R_HEAD + 3), mixed_hi)

                for n in range(NG):
                    def out_tail():
                        b = (n + 1) % 2
                        full(l, R_HEAD + R_MIX + n)
                        if n == 0:
                            act.wait_ge(proj_free, (NG + 1) * (l + 1))
                        squares(buf(b), n, 7 * l + 1)
                        for i in range(GT):
                            t = n * GT + i
                            s = act.activation(y[:, t, :], buf(b)[:, i * T:(i + 1) * T], ACT.Copy,
                                               scale=par[:, G_MIX_POST + t:G_MIX_POST + t + 1])
                        s.then_inc(buf_free[b], 1)
                        if n == 0:
                            ln_and_exp()
                    round_(l, R_HEAD + R_MIX + n, out_tail)

                guess_rstd(5 * l + 3, rstd[:, 0:T], T)

                def mlp_quarter(quarter, start=None):
                    first = quarter * (2 * NG) + (R_HEAD + R_MIX + R_OUT)

                    def squared(n):
                        act.wait_ge(f_float, l * 16 + quarter * 4 + (n + 1))
                        act.activation(group(mid_hi, n), slot[:, 4, :], ACT.Square).then_inc(f_hi_ready, 1)

                    if start:
                        round_(l, first, nothing, start)
                        round_(l, first + 1, lambda: squared(1),
                               {3: lambda: guess_rstd(5 * l + 4), 5: lambda: squared(0)})
                    for n in range(2 if start else 0, NG):
                        round_(l, first + n, lambda: squared(n))
                    for n in range(NG):
                        def down():
                            act.wait_ge(y_added, l * 16 + quarter * 4 + (n + 1))
                            squares(group(y, n), n, 7 * l + quarter + 3)
                        round_(l, first + NG + n, down)

                gained(0, G_MLP_PRE, 2 * l + 1)
                mlp_quarter(0, input_hooks(G_MLP_PRE, 7 * l + 2, 2 * l + 1))
                with act.Fori(1, NG) as quarter:
                    mlp_quarter(quarter)

                def y_times_gain(n):
                    for i in range(GT):
                        t = n * GT + i
                        s = act.activation(y[:, t, :], y[:, t, :], ACT.Copy,
                                           scale=par[:, G_MLP_POST + t:G_MLP_POST + t + 1])
                    s.then_inc(y_gained, 1)

                act.drain()
                y_times_gain(0)
                guess_rstd(5 * l + 5, rstd[:, 0:T], T)
                y_times_gain(1)
                y_times_gain(2)
                act.wait_ge(par_ready, l + 2)
                gained(0, G_MIX_PRE, 2 * l + 2)
                y_times_gain(3)

        @block.vector
        def _(dve):
            def split(l, rnd, m):
                dve.wait_ge(hi_ready, l * HALVES + rnd * 8 + (m + 1))
                dve.tensor_tensor(w_lo[:, m % 4, :], raw[:, m // 2, m % 2 * HALF:(m % 2 + 1) * HALF],
                                  w_hi[:, m % 4, :].bitcast(F32), ALU.subtract).then_inc(lo_ready, 1)

            def round_(l, rnd, tail, hooks={}):
                for m in range(8):
                    if m in hooks:
                        hooks[m]()
                    ahead = m + AHEAD
                    split(l, rnd + ahead // 8, ahead % 8)
                tail()

            def nothing():
                return None

            def full(l, rnd, c=3):
                dve.wait_ge(half_used, l * HALVES + rnd * 8 + (2 * (c + 1) + 4))

            def group(a, n):
                return a[:, n * GT:(n + 1) * GT, :].rearrange("p i t -> p (i t)")

            def flat(a):
                return a[:].rearrange("p i t -> p (i t)")

            def lo(out, exact, hi):
                return dve.tensor_tensor(out, exact, hi.bitcast(F32), ALU.subtract)

            def variance(count, eps, w=TV):
                dve.wait_ge(stat_logged, count)
                dve.tensor_scalar(var[:, 0:w], stat[:, 0:w], eps, None, ALU.add)

            def refine(count, r=rstd[:], w=TV):
                dve.wait_ge(rstd_guess, count)
                dve.scalar_tensor_tensor(newton[:, 0:w], r, -0.5, r, ALU.mult, ALU.mult)
                dve.drain()
                dve.tensor_tensor(newton[:, 0:w], newton[:, 0:w], var[:, 0:w], ALU.mult)
                dve.drain()
                dve.scalar_tensor_tensor(r, newton[:, 0:w], 1.5, r, ALU.add, ALU.mult)
                dve.drain()

            def scaled(out, b, scale=1.0):
                return dve.scalar_tensor_tensor(tiles(out), tiles(buf(b)), scale, over_tiles(rstd[:, 0:T]),
                                                ALU.mult, ALU.mult)

            def gained_lo(n, gain, norm, halves=(0, 1)):
                for half in halves:
                    dve.wait_ge(h_hi_ready, norm * 2 * NG + (2 * n + half + 1))
                    for i in range(2):
                        t = n * GT + 2 * half + i
                        s = dve.scalar_tensor_tensor(h_lo[:, t, :], x[:, t, :], par[:, gain + t:gain + t + 1],
                                                     h_hi[:, t, :].bitcast(F32), ALU.mult, ALU.subtract)
                    s.then_inc(h_ready, 1)

            def first_residual():
                for half in range(2):
                    ys = y[:, 2 * half:2 * half + 2, :]
                    dve.tensor_tensor(ys, ys, rstd[:, 0:T].unsqueeze(1).to_broadcast([P, 2, T]), ALU.mult)
                    dve.drain()
                    xs = x[:, 2 * half:2 * half + 2, :]
                    dve.tensor_tensor(xs, xs, ys, ALU.add).then_inc(x_ready, 1)
                dve.drain()

            def residual(n, scaled_before):
                dve.wait_ge(y_scaled, scaled_before + n)
                s = dve.tensor_tensor(group(x, n), group(x, n), group(y, n), ALU.add)
                if n < NG - 1:
                    s.then_inc(x_ready, 2)
                else:
                    s.then_inc(x_last_ready, 1)
                dve.drain()

            dve.wait_ge(params_landed, 16)
            dve.tensor_copy(par[:], par_all[:, 0:NPAR])
            dve.drain().then_inc(par_ready, 1)
            dve.sem_inc(x_ready, X_HALVES)
            gained_lo(0, G_MIX_PRE, 0, (0,))
            split(0, 0, 0)
            gained_lo(0, G_MIX_PRE, 0, (1,))
            split(0, 0, 1)
            split(0, 0, 2)

            with dve.Fori(0, DEPTH) as l:
                dve.tensor_copy(par[:, G_MLP_POST:NPAR], par_all[:, bass.ds(l * NPAR + G_MLP_POST, NT)])
                taps_done = [0]

                def taps(count):
                    for tap in range(taps_done[0], taps_done[0] + count):
                        for i in range(GT):
                            w = par[:, W_C + i * TAPS_C + tap:W_C + i * TAPS_C + tap + 1]
                            moved = glu_pad[:, i, tap:tap + T]
                            if tap == 0:
                                s = dve.tensor_scalar(conv_c[:, i, :], moved, w, par[:, B_C + i:B_C + i + 1],
                                                      ALU.mult, ALU.add)
                            else:
                                s = dve.scalar_tensor_tensor(conv_c[:, i, :], moved, w, conv_c[:, i, :],
                                                             ALU.mult, ALU.add)
                        if tap < TAPS_C - 1:
                            dve.drain()
                    taps_done[0] += count
                    if count and taps_done[0] == TAPS_C:
                        dve.drain().then_inc(conv_c_ready, 1)

                def first_variance():
                    variance(5 * l + 1, RMS_EPS)

                def glu_gate():
                    refine(5 * l + 1)
                    full(l, 0)
                    scaled(factor[:], 0).then_inc(buf_free[0], 1)
                    dve.drain().then_inc(glu_scaled, 1)

                def gate_times_rstd():
                    dve.memset(glu_pad[:, :, 0:PAD_C], 0.0)
                    dve.memset(cu_pad[:, :, 0:PAD_A], 0.0)
                    dve.wait_ge(gate_sig, l + 1)
                    dve.tensor_tensor(tiles(factor[:]), tiles(factor[:]), over_tiles(rstd[:, 0:T]), ALU.mult)
                    dve.drain()

                def glu():
                    full(l, 1)
                    dve.tensor_tensor(glu_pad[:, :, PAD_C:PAD_C + T], tiles(buf(1)), tiles(factor[:]),
                                      ALU.mult).then_inc(buf_free[1], 1)
                    dve.drain()
                    taps(TAP_PLAN[1][2])

                round_(l, 0, nothing, {0: lambda: gained_lo(1, G_MIX_PRE, 2 * l),
                                       1: lambda: gained_lo(2, G_MIX_PRE, 2 * l),
                                       3: lambda: gained_lo(3, G_MIX_PRE, 2 * l)})
                round_(l, 1, glu, {3: first_variance, 4: glu_gate, 6: gate_times_rstd})
                for i, (dst, half) in enumerate(((q, 0), (k, 0), (q, 1), (k, 1))):
                    early, late, last = TAP_PLAN[2 + i]

                    def take():
                        full(l, 2 + i)
                        scaled(group(dst, half), i % 2, SCALE if dst is q else 1.0).then_inc(buf_free[i % 2], 1)
                        taps(last)
                        dve.drain().then_inc(qk_ready, 1)
                    round_(l, 2 + i, take, {3: lambda: taps(early), 5: lambda: taps(late)})
                early, late, last = TAP_PLAN[6]
                round_(l, 6, lambda: taps(last), {3: lambda: taps(early), 5: lambda: taps(late)})

                def softplus(p):
                    dve.wait_ge(softplus_log, PAIRS * l + (p + 1))
                    for e in range(2):
                        dve.scalar_tensor_tensor(soft[:, e, :], scores[:, e, :], 0.0, att[:, e, :], ALU.max, ALU.add)
                    dve.drain()
                    dve.wait_ge(consts_landed, 16)
                    for e in range(2):
                        for at_ in (0, T):
                            s = dve.tensor_tensor(soft[:, e, at_:at_ + P], soft[:, e, at_:at_ + P],
                                                  consts[:, C_MASK:C_MASK + P], ALU.mult)
                    s.then_inc(softplus_ready, 1)

                def bounded(p):
                    dve.wait_ge(log_a_full, PAIRS * l + (p + 1))
                    dve.tensor_tensor(att[:], scores, consts[:, C_BOUND:C_BOUND + ZW].unsqueeze(1)
                                      .to_broadcast([P, 2, ZW]), ALU.min).then_inc(log_a_ready, 1)

                def heads_lo(p):
                    dve.wait_ge(yb_hi_ready, PAIRS * l + (p + 1))
                    pair = (slice(None), slice(2 * p, 2 * p + 2), slice(None))
                    lo(yb_lo[pair].rearrange("p i t -> p (i t)"), att_out,
                       yb_hi[pair].rearrange("p i t -> p (i t)")).then_inc(yb_ready, 1)

                def v1_late():
                    bounded(0)
                    taps(TAP_PLAN[7][1])

                def v1_tail():
                    heads_lo(0)
                    taps(TAP_PLAN[7][2])
                    assert taps_done[0] == TAPS_C

                round_(l, 7, v1_tail, {3: lambda: softplus(0), 5: v1_late})

                def sc_c_late():
                    bounded(1)
                    dve.wait_ge(mean_full, l + 1)
                    dve.tensor_tensor(conv_c[:], conv_c[:], over_tiles(stat[:, 0:T]),
                                      ALU.subtract).then_inc(centred, 1)

                def sc_c_tail():
                    full(l, 8)
                    scaled(factor[:], 0).then_inc(buf_free[0], 1)
                    heads_lo(1)

                round_(l, 8, sc_c_tail, {3: lambda: softplus(1), 5: sc_c_late})

                def sc_u_mid():
                    softplus(2)
                    dve.tensor_tensor(tiles(factor[:]), tiles(factor[:]), over_tiles(rstd[:, 0:T]), ALU.mult)
                    dve.drain()

                def sc_u_tail():
                    full(l, 9)
                    dve.tensor_tensor(cu_pad[:, :, PAD_A:PAD_A + T], tiles(buf(1)), tiles(factor[:]),
                                      ALU.mult).then_inc(buf_free[1], 1)
                    heads_lo(2)
                    variance(5 * l + 2, LN_EPS, T)
                    refine(5 * l + 2, ln_work[:, 0:T], T)
                    dve.tensor_tensor(conv_c[:], conv_c[:], over_tiles(ln_work[:, 0:T]), ALU.mult)
                    dve.drain()
                    for i in range(GT):
                        dve.tensor_scalar(conv_c[:, i, :], conv_c[:, i, :], par[:, G_LN + i:G_LN + i + 1],
                                          par[:, B_LN + i:B_LN + i + 1], ALU.mult, ALU.add)
                    dve.drain().then_inc(ln_ready, 1)

                round_(l, 9, sc_u_tail, {3: sc_u_mid, 5: lambda: bounded(2)})

                def short_conv(first, last):
                    for tap in range(first, last):
                        for i in range(GT):
                            w = par[:, W_A + i * TAPS_A + tap:W_A + i * TAPS_A + tap + 1]
                            moved = cu_pad[:, i, tap:tap + T]
                            if tap == 0:
                                dve.tensor_scalar(conv_a[:, i, :], moved, w, None, ALU.mult)
                            else:
                                dve.scalar_tensor_tensor(conv_a[:, i, :], moved, w, conv_a[:, i, :],
                                                         ALU.mult, ALU.add)
                        dve.drain()

                def sc_b_late():
                    bounded(3)
                    short_conv(1, 2)

                def sc_b_later():
                    short_conv(2, TAPS_A)
                    dve.tensor_tensor(conv_a[:], conv_a[:], over_tiles(rstd[:, 0:T]), ALU.mult)
                    dve.drain()

                def silu():
                    dve.wait_ge(ln_sig, l + 1)
                    dve.tensor_tensor(flat(conv_c), flat(conv_c), ln_work[:], ALU.mult)
                    dve.drain().then_inc(silu_ready, 1)

                def sc_b_tail():
                    full(l, 10)
                    dve.tensor_tensor(flat(conv_a), buf(0), flat(conv_a), ALU.mult).then_inc(buf_free[0], 1)
                    dve.drain().then_inc(ya_float, 1)
                    heads_lo(3)
                    dve.wait_ge(yc_hi_ready, l + 1)
                    lo(group(yc_lo, 0), flat(conv_c), group(yc_hi, 0))
                    dve.wait_ge(ya_hi_ready, l + 1)
                    lo(group(ya_lo, 0), flat(conv_a), group(ya_hi, 0)).then_inc(ya_ready, 1)
                    dve.drain().then_inc(proj_free, 1)

                round_(l, 10, sc_b_tail, {3: lambda: softplus(3), 4: lambda: short_conv(0, 1), 5: sc_b_late,
                                         6: sc_b_later, 7: silu})

                with dve.Fori(0, NG) as j:
                    for i, b in enumerate((1, 0, 1)):
                        def gate():
                            full(l, j * 4 + (R_HEAD + i))
                            scaled(slot[:, i, :], b).then_inc(buf_free[b], 1)
                            dve.drain().then_inc(gate_scaled, 1)
                        round_(l, j * 4 + (R_HEAD + i), gate)

                    def branch_a():
                        dve.wait_ge(gate_ready, 3 * NG * l + j * 3 + 3)
                        full(l, j * 4 + (R_HEAD + 3), 0)
                        dve.tensor_tensor(slot[:, 3, :], buf(0), slot[:, 0, :], ALU.mult).then_inc(buf_free[0], 1)
                        dve.drain()

                    def branch_c():
                        full(l, j * 4 + (R_HEAD + 3), 1)
                        dve.tensor_tensor(slot[:, 4, :], buf(2), slot[:, 2, :], ALU.mult)
                        dve.drain()
                        dve.tensor_tensor(slot[:, 3, :], slot[:, 3, :], slot[:, 4, :], ALU.add)
                        dve.drain()

                    def branch_b():
                        full(l, j * 4 + (R_HEAD + 3))
                        dve.tensor_tensor(slot[:, 4, :], buf(3), slot[:, 1, :], ALU.mult)
                        dve.drain()
                        dve.tensor_tensor(slot[:, 3, :], slot[:, 3, :], slot[:, 4, :], ALU.add)
                        dve.drain().then_inc(mixed_float, 1)
                        dve.wait_ge(mixed_hi_ready, NG * l + j + 1)
                        lo(mid_lo[:, bass.ds(j * GT, GT), :], tiles(slot[:, 3, :]),
                           mid_hi[:, bass.ds(j * GT, GT), :]).then_inc(mixed_ready, 1)
                        dve.drain().then_inc(proj_free, 1)

                    round_(l, j * 4 + (R_HEAD + 3), branch_b, {3: branch_a, 5: branch_c})

                with dve.Fori(0, NG) as n:
                    round_(l, n + (R_HEAD + R_MIX), nothing)
                variance(5 * l + 3, RMS_EPS, T)
                refine(5 * l + 3, rstd[:, 0:T], T)

                dve.drain().then_inc(rstd_ready, 1)

                def residuals(gain, norm, scaled_before):
                    first_residual()
                    gained_lo(0, gain, norm, (0,))
                    residual(1, scaled_before)
                    gained_lo(0, gain, norm, (1,))
                    residual(2, scaled_before)

                def first_groups():
                    dve.wait_ge(buf_free[0], l * USES[0] + 17)
                    residuals(G_MLP_PRE, 2 * l + 1, 6 * l)
                    gained_lo(1, G_MLP_PRE, 2 * l + 1)

                def mlp_quarter(quarter, start=None):
                    first = quarter * (2 * NG) + (R_HEAD + R_MIX + R_OUT)

                    def relu(n):
                        full(l, first + n)
                        b = (n + 1) % 2
                        dve.scalar_tensor_tensor(tiles(slot[:, 4, :]), tiles(buf(b)), 0.0,
                                                 over_tiles(rstd[:, 0:T]), ALU.max,
                                                 ALU.mult).then_inc(buf_free[b], 1)
                        dve.drain().then_inc(f_float, 1)

                    def squared(n):
                        dve.wait_ge(f_hi_ready, l * 16 + quarter * 4 + (n + 1))
                        dve.tensor_tensor(slot[:, 4, :], slot[:, 4, :], slot[:, 4, :], ALU.mult)
                        dve.drain()
                        lo(group(mid_lo, n), slot[:, 4, :], group(mid_hi, n)).then_inc(f_ready, 1)
                        dve.drain()

                    def first_relu():
                        refine(5 * l + 4)
                        relu(0)

                    def clear_y(n):
                        dve.memset(group(y, n), 0.0)
                        dve.drain()

                    if start:
                        round_(l, first, nothing, start)
                        round_(l, first + 1, lambda: (relu(1), squared(1)),
                               {3: lambda: variance(5 * l + 4, RMS_EPS), 4: first_relu, 6: lambda: squared(0)})
                    for n in range(2 if start else 0, NG):
                        round_(l, first + n, lambda: (relu(n), squared(n)),
                               {3: lambda: clear_y(2 * n - 4), 5: lambda: clear_y(2 * n - 3)} if start else {})
                    for n in range(NG):
                        def down():
                            b = (n + 1) % 2
                            full(l, first + NG + n)
                            dve.tensor_tensor(group(y, n), group(y, n), buf(b), ALU.add).then_inc(buf_free[b], 1)
                            dve.drain().then_inc(y_added, 1)
                        round_(l, first + NG + n, down)

                mlp_quarter(0, {0: first_groups, 1: lambda: gained_lo(2, G_MLP_PRE, 2 * l + 1),
                                3: lambda: gained_lo(3, G_MLP_PRE, 2 * l + 1)})
                with dve.Fori(1, NG) as quarter:
                    mlp_quarter(quarter)

                dve.tensor_copy(par[:, 0:G_MLP_POST], par_all[:, bass.ds((l + 1) * NPAR, G_MLP_POST)])
                dve.drain().then_inc(par_ready, 1)
                variance(5 * l + 5, RMS_EPS, T)
                refine(5 * l + 5, rstd[:, 0:T], T)
                dve.drain().then_inc(rstd_ready, 1)
                dve.wait_ge(y_gained, NG * l + 1)
                residuals(G_MIX_PRE, 2 * l + 2, 6 * l + 3)
                residual(NG - 1, 6 * l + 3)

        @block.tensor
        def _(pe):
            pe.sem_inc(half_used, 4)
            pe.sem_inc(buf_free[0], 1)
            pe.sem_inc(buf_free[1], 1)

            def weights(c, kk, first, count):
                at_ = (kk % 2) * GT * P + first
                return slice(None), (2 * c + kk // 2) % 4, slice(at_, at_ + count)

            def chunk(n, c, out, hi, lo, tile0, first, last, h_before=None):
                for kk in range(KK):
                    if kk % 2 == 0:
                        if h_before is not None:
                            pe.wait_ge(h_ready, h_before + (kk // 2 + 1))
                        pe.wait_ge(lo_ready, 2 * n + (kk // 2 + 1))
                    for i in range(GT):
                        w = weights(c, kk, i * P, P)
                        o = out[:, i * T:(i + 1) * T]
                        t = tile0 + kk
                        pe.matmul(o, w_hi[w], hi[:, t, :], start=first and kk == 0 and i % 2 == 0, stop=False,
                                  skip_group_check=True)
                        pe.matmul(o, w_hi[w], lo[:, t, :], start=False, stop=False, skip_group_check=True)
                        s = pe.matmul(o, w_lo[w], hi[:, t, :], start=False, stop=last and kk == KK - 1,
                                      skip_group_check=True)
                    if kk % 2:
                        s.then_inc(half_used, 1)

            def round_(l, rnd, b, use, hi, lo, ready=None, between=None, h_before=None):
                pe.wait_ge(buf_free[b], l * USES[b] + use + 1)
                n = l * CHUNKS + rnd * 4
                for c in range(4):
                    if ready:
                        pe.wait_ge(ready[0], ready[1] + (c + 1))
                    chunk(n + c, c, buf(b), hi, lo, c * KK, c == 0, c == 3,
                          None if h_before is None else h_before + 2 * c)
                    if between:
                        between(c)

            def statistics(source, done):
                for i in range(GT):
                    s = pe.matmul(stat[:, 0:T], consts[:, C_LN:C_LN + P], source[:, i * T:(i + 1) * T],
                                  start=i == 0, stop=i == GT - 1)
                s.then_inc(done, 1)

            def norm_before(l, sums):
                pe.wait_ge(consts_landed, 16)
                pe.wait_ge(sum_ready, 7 * l + (sums + 1))
                for i in range(GT):
                    pe.matmul(stat[:, 0:T], consts[:, C_RMS:C_RMS + P], slot[:, 0, i * T:(i + 1) * T],
                              start=i == 0, stop=False, skip_group_check=True)
                for t in range(2):
                    for i in range(GT):
                        s = pe.matmul(stat[:, T + t:T + t + 1], slot[:, 0, i * T + t * P:i * T + (t + 1) * P],
                                      consts[:, C_RMS:C_RMS + 1], start=False, stop=i == GT - 1,
                                      skip_group_check=True)
                s.then_inc(stat_full, 1)

            def norm_after(l, sums, squared):
                pe.wait_ge(sum_ready, 7 * l + (sums + 1))
                for n in (0, NG - 1):
                    if n:
                        pe.wait_ge(squares_ready, l * 28 + squared)
                    for i in range(GT):
                        s = pe.matmul(stat[:, 0:T], consts[:, C_RMS:C_RMS + P], slot[:, n, i * T:(i + 1) * T],
                                      start=n == 0 and i == 0, stop=n > 0 and i == GT - 1)
                s.then_inc(stat_full, 1)

            with pe.Fori(0, DEPTH) as l:
                round_(l, 0, 0, 0, h_hi, h_lo, h_before=16 * l)
                round_(l, 1, 1, 0, h_hi, h_lo,
                       between=lambda c: norm_before(l, 1) if c == 0 else None)
                with pe.Fori(1, 3) as i:
                    for b in range(2):
                        round_(l, i * 2 + b, b, i, h_hi, h_lo)

                def attention(c, p):
                    if c == 0:
                        pe.wait_ge(qk_ready, 4 * l + 4)
                        for e in range(2):
                            hd = 2 * p + e
                            pe.matmul(scores[:, e, 0:T], k[:, hd, 0:P], q[:, hd, :], start=True, stop=False,
                                      skip_group_check=True)
                            s = pe.matmul(scores[:, e, T:ZW], k[:, hd, P:T], q[:, hd, P:T], start=False,
                                          stop=False, skip_group_check=True)
                        s.then_inc(scores_full, 1)
                    if c == 1:
                        pe.wait_ge(softplus_ready, PAIRS * l + (p + 1))
                        for e in range(2):
                            up_to, all_ = consts[:, C_NU:C_NU + P], consts[:, C_NO:C_NO + P]
                            pe.matmul(scores[:, e, 0:T], up_to, soft[:, e, 0:T], start=False, stop=False,
                                      skip_group_check=True)
                            pe.matmul(scores[:, e, P:T], all_, soft[:, e, T:ZW], start=False, stop=True,
                                      skip_group_check=True)
                            s = pe.matmul(scores[:, e, T:ZW], up_to, soft[:, e, T:ZW], start=False, stop=True,
                                          skip_group_check=True)
                        s.then_inc(log_a_full, 1)
                    if c == 2:
                        pe.wait_ge(att_ready, PAIRS * l + (p + 1))
                        pe.wait_ge(v_ready, 2 * l + (1 if p < PAIRS // 2 else 2))
                        if p:
                            pe.wait_ge(yb_ready, PAIRS * l + p)
                        for e in range(2):
                            hd = 2 * p + e
                            pe.matmul(att_out[:, e * T:(e + 1) * T], v[:, 0, hd * HD:(hd + 1) * HD],
                                      att[:, e, 0:T], start=True, stop=False, skip_group_check=True)
                            s = pe.matmul(att_out[:, e * T + P:(e + 1) * T], v[:, 1, hd * HD:(hd + 1) * HD],
                                          att[:, e, T:ZW], start=False, stop=True, skip_group_check=True)
                        s.then_inc(out_full, 1)

                for half in range(2):
                    pe.wait_ge(buf_free[half], l * USES[half] + 4)
                    for c in range(4):
                        n = l * CHUNKS + (6 + half) * 4 + c
                        for kk in range(KK):
                            if kk % 2 == 0:
                                pe.wait_ge(lo_ready, 2 * n + (kk // 2 + 1))
                            w = weights(c, kk, 0, GT * P)
                            for t in range(2):
                                h = (slice(None), c * KK + kk, slice(t * P, (t + 1) * P))
                                o = ps[:, 2 * half + t, :]
                                pe.matmul(o, h_hi[h], w_hi[w], start=c == 0 and kk == 0, stop=False,
                                          skip_group_check=True)
                                pe.matmul(o, h_hi[h], w_lo[w], start=False, stop=False, skip_group_check=True)
                                s = pe.matmul(o, h_lo[h], w_hi[w], start=False, stop=c == 3 and kk == KK - 1,
                                              skip_group_check=True)
                            if kk % 2:
                                s.then_inc(half_used, 1)
                        if half == 1:
                            attention(c, 0)

                def beside_sc_c(c):
                    attention(c, 1)
                    if c == 1:
                        pe.wait_ge(conv_c_ready, l + 1)
                        statistics(conv_c[:].rearrange("p i t -> p (i t)"), mean_full)

                def beside_sc_u(c):
                    attention(c, 2)
                    if c == 0:
                        pe.wait_ge(ln_squared, l + 1)
                        statistics(ln_work, stat_full)

                round_(l, 8, 0, 4, h_hi, h_lo, between=beside_sc_c)
                round_(l, 9, 1, 4, h_hi, h_lo, between=beside_sc_u)
                round_(l, 10, 0, 5, h_hi, h_lo, between=lambda c: attention(c, 3))

                with pe.Fori(0, NG) as j:
                    for i, b in enumerate((1, 0, 1)):
                        round_(l, j * 4 + (R_HEAD + i), b, j * 2 + ((6, 5)[b] + i // 2), h_hi, h_lo)
                    n = l * CHUNKS + j * 16 + (4 * (R_HEAD + 3))
                    pe.wait_ge(ya_ready, l + 1)
                    pe.wait_ge(buf_free[0], l * USES[0] + j * 2 + 8)
                    chunk(n, 0, buf(0), ya_hi, ya_lo, 0, True, True)
                    pe.wait_ge(proj_free, (NG + 1) * l + j + 1)
                    chunk(n + 1, 1, buf(2), yc_hi, yc_lo, 0, True, True)
                    for c in range(2):
                        chunk(n + (2 + c), 2 + c, buf(3), yb_hi, yb_lo, c * KK, c == 0, c == 1)

                with pe.Fori(0, 2) as i:
                    for e, b in enumerate((1, 0)):
                        round_(l, i * 2 + (R_HEAD + R_MIX + e), b, i + (14, 13)[b], mid_hi, mid_lo,
                               (mixed_ready, NG * l))
                norm_after(l, 2, 8)

                def mlp_quarter(quarter, first_up):
                    first = quarter * (2 * NG) + (R_HEAD + R_MIX + R_OUT)
                    up = [(i, e, b) for i in range(2) for e, b in enumerate((1, 0))]
                    for i, e, b in up[first_up:]:
                        round_(l, first + (i * 2 + e), b, quarter * 4 + (i + (16, 15)[b]), h_hi, h_lo,
                               between=(lambda c: norm_before(l, 3) if c == 0 else None) if first_up and i == 0
                               else None)
                    with pe.Fori(0, 2) as i:
                        for e, b in enumerate((1, 0)):
                            round_(l, first + i * 2 + (NG + e), b, quarter * 4 + i + (18, 17)[b], mid_hi, mid_lo,
                                   (f_ready, l * 16 + quarter * 4))

                round_(l, R_HEAD + R_MIX + R_OUT, 1, 15, h_hi, h_lo, h_before=16 * l + 8)
                mlp_quarter(0, 1)
                with pe.Fori(1, NG) as quarter:
                    mlp_quarter(quarter, 0)
                norm_after(l, 7, 28)


def constants():
    s, t = np.arange(P)[:, None], np.arange(P)[None, :]
    c = np.zeros((P, NCONST), np.float32)
    c[:, C_RMS:C_RMS + P] = 1.0 / D
    c[:, C_LN:C_LN + P] = 1.0 / D_CF
    c[:, C_NU:C_NU + P] = np.where(s >= t, -1.0, 0.0)
    c[:, C_NO:C_NO + P] = -1.0
    c[:, C_MASK:C_MASK + P] = np.where(s < t, 1.0, 0.0)
    c[:, C_RMS_EPS], c[:, C_LN_EPS] = RMS_EPS, LN_EPS
    c[:, C_BOUND:C_BOUND + ZW] = BIG
    for at in (0, T):
        c[:, C_BOUND + at:C_BOUND + at + P] = np.where(s < t, BIG, -BIG)
    return c


def chunks(w):
    kdim, n = w.shape
    return w.reshape(kdim // (KK * P), KK, P, n // (GT * P), GT * P).transpose(3, 0, 2, 1, 4)


def weight_stream(w_in, proj_a, proj_b, proj_c, w_o, w_up, w_down):
    stream = np.empty((DEPTH * CHUNKS, P, KK, GT * P), np.float32)
    at = 0

    def put(c):
        nonlocal at
        stream[at:at + c.shape[0]] = c
        at += c.shape[0]

    sc = 3 * D_ATT // (GT * P)
    glu, gates = sc + 3 * D_SC // (GT * P), sc + (3 * D_SC + 2 * D_CF) // (GT * P)
    for l in range(DEPTH):
        win = chunks(w_in[l])
        for g in (glu + 1, glu, 0, 2, 1, 3, 4, 5, sc + 1, sc + 2, sc):
            put(win[g])
        pa, pb, pc = chunks(proj_a[l]), chunks(proj_b[l]), chunks(proj_c[l])
        for j in range(NG):
            for branch in range(3):
                put(win[gates + branch * NG + j])
            put(pa[j])
            put(pc[j])
            put(pb[j])
        for g in chunks(w_o[l]):
            put(g)
        up, down = chunks(w_up[l]), chunks(w_down[l])
        for quarter in range(NG):
            for n in range(NG):
                put(up[quarter * NG + n])
            for n in range(NG):
                put(down[n, quarter * NG:(quarter + 1) * NG])
    assert at == DEPTH * CHUNKS
    return stream.reshape(DEPTH * CHUNKS, P, CW)


def by_partition(a):
    a = np.asarray(a)
    return np.moveaxis(a.reshape(*a.shape[:-1], a.shape[-1] // P, P), -1, 0)


def kernel(x, ln_mix_pre, ln_mix_post, ln_mlp_pre, ln_mlp_post, w_in, conv_a_w, proj_a, proj_b, conv_c_w,
           conv_c_b, norm_c_g, norm_c_b, proj_c, w_o, w_up, w_down):
    import concourse.bacc as bacc
    from concourse.bass_utils import run_bass_kernel_spmd

    params = np.zeros((P, DEPTH + 1, NPAR), np.float32)
    for at, a in ((G_MIX_PRE, ln_mix_pre), (G_MIX_POST, ln_mix_post), (G_MLP_PRE, ln_mlp_pre),
                  (G_MLP_POST, ln_mlp_post), (B_C, conv_c_b), (G_LN, norm_c_g), (B_LN, norm_c_b)):
        a = by_partition(a)
        params[:, :DEPTH, at:at + a.shape[-1]] = a
    for at, a in ((W_A, conv_a_w), (W_C, conv_c_w)):
        a = by_partition(a)
        params[:, :DEPTH, at:at + a.shape[2] * a.shape[3]] = a.transpose(0, 1, 3, 2).reshape(P, DEPTH, -1)
    arrays = {
        "w_stream": weight_stream(*(np.asarray(a) for a in (w_in, proj_a, proj_b, proj_c, w_o, w_up, w_down))),
        "x_in": np.ascontiguousarray(by_partition(np.asarray(x)[0]).transpose(0, 2, 1)),
        "params_in": params.reshape(P, (DEPTH + 1) * NPAR),
        "consts_in": constants(),
    }
    nc = bacc.Bacc("TRN2", target_bir_lowering=False, num_devices=1)
    args = [nc.dram_tensor(name, a.shape, F32, kind="ExternalInput").ap() for name, a in arrays.items()]
    y_out = nc.dram_tensor("y_out", (P, NT, T), F32, kind="ExternalOutput").ap()
    build(nc, *args, y_out)
    result = run_bass_kernel_spmd(nc, [arrays], core_ids=[0]).results[0]["y_out"]
    return result.transpose(2, 1, 0).reshape(1, T, D)
```
